# Optimizing a Trainium2 kernel written in Bass

```python
import math
import jax, jax.numpy as jnp
from jax import lax
import numpy as np

D_MODEL = 1024
BATCH = 1
SEQ = 256
DEPTH = 1
DEC_BATCH = 8
DEC_SEQ = 1
PAST_LEN = 2048
PAGE_SIZE = 128

D_MIX = D_MODEL
CONV_CH = D_MIX // 2
CONV_WIDTH = 31
GDN_HEADS = 4
GDN_DK = 128
GDN_DV = 128
GDN_QK = GDN_HEADS * GDN_DK
GDN_V = GDN_HEADS * GDN_DV
QKV_CH = 2 * GDN_QK + GDN_V
SHORT_CONV = 4
GDN_CHUNK = 64
N_MEM = 256
X_HEADS = 4
X_HEAD_DIM = D_MODEL // X_HEADS
N_EXPERTS = 32
TOP_K = 4
D_EXPERT = D_MODEL
SWIGLU_LIMIT = 7.0
SWIGLU_ALPHA = 1.702
NORM_EPS = 1e-6
OFF_QKV = 2 * CONV_CH
OFF_Z = OFF_QKV + QKV_CH
OFF_A = OFF_Z + GDN_V
OFF_B = OFF_A + GDN_HEADS
P_IN = OFF_B + GDN_HEADS

kernel_name = 'hymba_conformer_gdn_moe_step'

def rmsnorm(x, g):
    xf = x.astype(jnp.float32)
    y = xf * lax.rsqrt(jnp.mean(xf * xf, axis=-1, keepdims=True) + NORM_EPS)
    return (y * g.astype(jnp.float32)).astype(x.dtype)

def layernorm(x, g, b):
    xf = x.astype(jnp.float32)
    mu = jnp.mean(xf, axis=-1, keepdims=True)
    var = jnp.mean(jnp.square(xf - mu), axis=-1, keepdims=True)
    y = (xf - mu) * lax.rsqrt(var + NORM_EPS) * g.astype(jnp.float32) + b.astype(jnp.float32)
    return y.astype(x.dtype)

def l2norm(x):
    return x * lax.rsqrt(jnp.sum(x * x, axis=-1, keepdims=True) + NORM_EPS)

def causal_depthwise(xh, w):
    return lax.conv_general_dilated(xh, w[:, None, :].astype(xh.dtype), (1,), 'VALID',
                                    dimension_numbers=('NWC', 'WIO', 'NWC'),
                                    feature_group_count=xh.shape[-1])

def conformer_mixer(u_glu, hist, w_dw, b_dw, ln_g, ln_b):
    glu = u_glu[..., :CONV_CH] * jax.nn.sigmoid(u_glu[..., CONV_CH:])
    xh = jnp.concatenate([hist.astype(glu.dtype), glu], axis=1)
    c = causal_depthwise(xh, w_dw) + b_dw.astype(glu.dtype)
    c = layernorm(c, ln_g, ln_b)
    return jax.nn.silu(c), xh[:, -(CONV_WIDTH - 1):]

def gdn_inputs(u, hist, w_sc, a_log, dt_bias):
    n, t, _ = u.shape
    xh = jnp.concatenate([hist.astype(u.dtype), u[..., OFF_QKV:OFF_Z]], axis=1)
    qkv = jax.nn.silu(causal_depthwise(xh, w_sc)).astype(jnp.float32)
    q = l2norm(qkv[..., :GDN_QK].reshape(n, t, GDN_HEADS, GDN_DK)) * (GDN_DK ** -0.5)
    k = l2norm(qkv[..., GDN_QK:2 * GDN_QK].reshape(n, t, GDN_HEADS, GDN_DK))
    v = qkv[..., 2 * GDN_QK:].reshape(n, t, GDN_HEADS, GDN_DV)
    a = u[..., OFF_A:OFF_B].astype(jnp.float32)
    b = u[..., OFF_B:P_IN].astype(jnp.float32)
    g = -jnp.exp(a_log.astype(jnp.float32)) * jax.nn.softplus(a + dt_bias.astype(jnp.float32))
    beta = jax.nn.sigmoid(b)
    return q, k, v, g, beta, xh[:, -(SHORT_CONV - 1):]

def gdn_chunked(q, k, v, g, beta, s0):
    n, t, h, _ = q.shape
    dv = v.shape[-1]
    nc = t // GDN_CHUNK

    def chunks(a):
        a = a.reshape((n, nc, GDN_CHUNK, h) + a.shape[3:])
        return jnp.moveaxis(jnp.moveaxis(a, 1, 0), 3, 2)

    qc, kc, vc = chunks(q), chunks(k), chunks(v)
    gc = jnp.cumsum(chunks(g), axis=-1)
    bc = chunks(beta)
    causal = jnp.tril(jnp.ones((GDN_CHUNK, GDN_CHUNK), dtype=bool))
    strict = jnp.tril(jnp.ones((GDN_CHUNK, GDN_CHUNK), dtype=bool), k=-1)
    diff = gc[..., :, None] - gc[..., None, :]
    decay = jnp.where(causal, jnp.exp(jnp.where(causal, diff, 0.0)), 0.0)
    k_beta = kc * bc[..., None]
    v_beta = vc * bc[..., None]
    lower = jnp.where(strict, jnp.einsum('...ik,...jk->...ij', k_beta, kc) * decay, 0.0)
    eye = jnp.eye(GDN_CHUNK, dtype=jnp.float32)
    t_inv = lax.linalg.triangular_solve(eye + lower, jnp.broadcast_to(eye, lower.shape),
                                        left_side=True, lower=True, unit_diagonal=True)
    u = t_inv @ v_beta
    w = t_inv @ (k_beta * jnp.exp(gc)[..., None])
    intra = jnp.where(causal, jnp.einsum('...ik,...jk->...ij', qc, kc) * decay, 0.0)

    def step(s, inp):
        q_c, k_c, u_c, w_c, g_c, a_c = inp
        v_new = u_c - w_c @ s
        o = (q_c * jnp.exp(g_c)[..., None]) @ s + a_c @ v_new
        g_last = g_c[..., -1:]
        s = s * jnp.exp(g_last)[..., None] + jnp.einsum(
            'nhck,nhcv->nhkv', k_c * jnp.exp(g_last - g_c)[..., None], v_new)
        return s, o

    s_fin, o = lax.scan(step, s0, (qc, kc, u, w, gc, intra))
    o = jnp.moveaxis(jnp.moveaxis(o, 2, 3), 0, 1).reshape(n, t, h, dv)
    return o, s_fin

def gdn_recurrent(q, k, v, g, beta, s0):
    def step(s, inp):
        q_t, k_t, v_t, g_t, b_t = inp
        s = s * jnp.exp(g_t)[..., None, None]
        v_t = (v_t - jnp.einsum('nhkv,nhk->nhv', s, k_t)) * b_t[..., None]
        s = s + jnp.einsum('nhk,nhv->nhkv', k_t, v_t)
        return s, jnp.einsum('nhkv,nhk->nhv', s, q_t)

    xs = tuple(jnp.moveaxis(a, 1, 0) for a in (q, k, v, g, beta))
    s_fin, o = lax.scan(step, s0, xs)
    return jnp.moveaxis(o, 0, 1), s_fin

def memory_kv(mem, g_mem, w_mk, w_mv):
    n = mem.shape[0]
    m = rmsnorm(mem, g_mem)
    mk = (m @ w_mk).reshape(n, N_MEM, X_HEADS, X_HEAD_DIM)
    mv = (m @ w_mv).reshape(n, N_MEM, X_HEADS, X_HEAD_DIM)
    return mk, mv

def cross_attn(h, mem_k, mem_v, w_q, w_o):
    n, t, _ = h.shape
    q = (h @ w_q).reshape(n, t, X_HEADS, X_HEAD_DIM)
    s = jnp.einsum('bthd,bmhd->bhtm', q, mem_k.astype(q.dtype)).astype(jnp.float32) * (X_HEAD_DIM ** -0.5)
    p = jax.nn.softmax(s, axis=-1).astype(h.dtype)
    o = jnp.einsum('bhtm,bmhd->bthd', p, mem_v.astype(h.dtype)).reshape(n, t, X_HEADS * X_HEAD_DIM)
    return (o @ w_o).astype(h.dtype)

def moe(h, w_r, b_r, w_gu, b_gu, w_dn, b_dn):
    n, t, d = h.shape
    ht = h.reshape(n * t, d)
    logits = (ht @ w_r + b_r).astype(jnp.float32)
    top_val, top_idx = lax.top_k(logits, TOP_K)
    gate = jax.nn.softmax(top_val, axis=-1)
    dense_gate = jnp.einsum('mk,mke->me', gate, jax.nn.one_hot(top_idx, N_EXPERTS, dtype=jnp.float32))
    out = jnp.zeros((n * t, d), jnp.float32)
    for e in range(N_EXPERTS):
        gu = ht @ w_gu[e] + b_gu[e]
        x_glu = jnp.minimum(gu[:, :D_EXPERT], SWIGLU_LIMIT)
        x_lin = jnp.clip(gu[:, D_EXPERT:], -SWIGLU_LIMIT, SWIGLU_LIMIT)
        act = x_glu * jax.nn.sigmoid(SWIGLU_ALPHA * x_glu) * (x_lin + 1.0)
        out = out + dense_gate[:, e:e + 1] * (act @ w_dn[e] + b_dn[e]).astype(jnp.float32)
    return out.reshape(n, t, d).astype(h.dtype)

def decoder_layer(x, mem_k, mem_v, conv_hist, sc_hist, s0, p, chunked):
    n, t, _ = x.shape
    h = rmsnorm(x, p['g_mix'])
    u = h @ p['w_in']
    conv_out, conv_new = conformer_mixer(u[..., :OFF_QKV] + p['b_glu'], conv_hist,
                                         p['w_dw'], p['b_dw'], p['ln_g'], p['ln_b'])
    q, k, v, g, beta, sc_new = gdn_inputs(u, sc_hist, p['w_sc'], p['a_log'], p['dt_bias'])
    if chunked:
        o, s_new = gdn_chunked(q, k, v, g, beta, s0)
    else:
        o, s_new = gdn_recurrent(q, k, v, g, beta, s0)
    z = u[..., OFF_Z:OFF_A].reshape(n, t, GDN_HEADS, GDN_DV).astype(jnp.float32)
    o = rmsnorm(o, p['g_onorm']) * jax.nn.silu(z)
    mixed = jnp.concatenate([conv_out, o.reshape(n, t, GDN_V).astype(x.dtype)], axis=-1) @ p['w_out']
    x = x + mixed
    x = x + cross_attn(rmsnorm(x, p['g_xattn']), mem_k, mem_v, p['w_xq'], p['w_xo'])
    x = x + moe(rmsnorm(x, p['g_moe']), p['w_router'], p['b_router'], p['w_gu'], p['b_gu'],
                p['w_dn'], p['b_dn'])
    return x, conv_new, sc_new, s_new

def setup_inputs(seed: int = 0) -> dict:
    key = jax.random.key(seed)
    ks = iter(jax.random.split(key, 48))

    def nrm(shape, scale):
        return scale * jax.random.normal(next(ks), shape, jnp.float32)

    def gain(shape):
        return 1.0 + nrm(shape, 0.02)

    a_log = jnp.log(jax.random.uniform(next(ks), (DEPTH, GDN_HEADS), jnp.float32, 1.0, 16.0))
    dt = jnp.exp(jax.random.uniform(next(ks), (DEPTH, GDN_HEADS), jnp.float32,
                                    math.log(1e-3), math.log(1e-1)))
    dt_bias = dt + jnp.log(-jnp.expm1(-dt))
    return {
        'x_prompt': nrm((BATCH, SEQ, D_MODEL), 1.0),
        'mem_prompt': nrm((BATCH, N_MEM, D_MODEL), 1.0),
        'x_sample': nrm((DEC_BATCH, DEC_SEQ, D_MODEL), 1.0),
        'state_conformer_conv': nrm((DEPTH, DEC_BATCH, CONV_WIDTH - 1, CONV_CH), 0.5),
        'state_gdn_conv': nrm((DEPTH, DEC_BATCH, SHORT_CONV - 1, QKV_CH), 1.0),
        'state_gdn': nrm((DEPTH, DEC_BATCH, GDN_HEADS, GDN_DK, GDN_DV), 0.2),
        'cache_mem_k': nrm((DEPTH, DEC_BATCH, N_MEM, X_HEADS, X_HEAD_DIM), 1.0),
        'cache_mem_v': nrm((DEPTH, DEC_BATCH, N_MEM, X_HEADS, X_HEAD_DIM), 1.0),
        'w_in': nrm((DEPTH, D_MODEL, P_IN), D_MODEL ** -0.5),
        'b_glu': nrm((DEPTH, 2 * CONV_CH), 0.02),
        'w_dw': nrm((DEPTH, CONV_WIDTH, CONV_CH), CONV_WIDTH ** -0.5),
        'b_dw': nrm((DEPTH, CONV_CH), 0.02),
        'ln_g': gain((DEPTH, CONV_CH)),
        'ln_b': nrm((DEPTH, CONV_CH), 0.02),
        'w_sc': nrm((DEPTH, SHORT_CONV, QKV_CH), SHORT_CONV ** -0.5),
        'a_log': a_log,
        'dt_bias': dt_bias,
        'g_onorm': gain((DEPTH, GDN_DV)),
        'w_out': nrm((DEPTH, D_MIX, D_MODEL), D_MIX ** -0.5),
        'g_mix': gain((DEPTH, D_MODEL)),
        'g_xattn': gain((DEPTH, D_MODEL)),
        'g_mem': gain((DEPTH, D_MODEL)),
        'w_xq': nrm((DEPTH, D_MODEL, D_MODEL), D_MODEL ** -0.5),
        'w_mk': nrm((DEPTH, D_MODEL, D_MODEL), D_MODEL ** -0.5),
        'w_mv': nrm((DEPTH, D_MODEL, D_MODEL), D_MODEL ** -0.5),
        'w_xo': nrm((DEPTH, D_MODEL, D_MODEL), D_MODEL ** -0.5),
        'g_moe': gain((DEPTH, D_MODEL)),
        'w_router': nrm((DEPTH, D_MODEL, N_EXPERTS), D_MODEL ** -0.5),
        'b_router': nrm((DEPTH, N_EXPERTS), 0.01),
        'w_gu': nrm((DEPTH, N_EXPERTS, D_MODEL, 2 * D_EXPERT), D_MODEL ** -0.5),
        'b_gu': nrm((DEPTH, N_EXPERTS, 2 * D_EXPERT), 0.01),
        'w_dn': nrm((DEPTH, N_EXPERTS, D_EXPERT, D_MODEL), D_EXPERT ** -0.5),
        'b_dn': nrm((DEPTH, N_EXPERTS, D_MODEL), 0.01),
        'g_final': gain((D_MODEL,)),
    }

def reference(x_prompt, mem_prompt, x_sample, state_conformer_conv, state_gdn_conv, state_gdn,
              cache_mem_k, cache_mem_v, w_in, b_glu, w_dw, b_dw, ln_g, ln_b, w_sc, a_log, dt_bias,
              g_onorm, w_out, g_mix, g_xattn, g_mem, w_xq, w_mk, w_mv, w_xo, g_moe, w_router,
              b_router, w_gu, b_gu, w_dn, b_dn, g_final):
    yp, ys = x_prompt, x_sample
    nb = x_prompt.shape[0]
    pc, pg, ps, pk, pv, sc, sg, ss = [], [], [], [], [], [], [], []
    for l in range(DEPTH):
        p = {'w_in': w_in[l], 'b_glu': b_glu[l], 'w_dw': w_dw[l], 'b_dw': b_dw[l],
             'ln_g': ln_g[l], 'ln_b': ln_b[l], 'w_sc': w_sc[l], 'a_log': a_log[l],
             'dt_bias': dt_bias[l], 'g_onorm': g_onorm[l], 'w_out': w_out[l], 'g_mix': g_mix[l],
             'g_xattn': g_xattn[l], 'w_xq': w_xq[l], 'w_xo': w_xo[l], 'g_moe': g_moe[l],
             'w_router': w_router[l], 'b_router': b_router[l], 'w_gu': w_gu[l], 'b_gu': b_gu[l],
             'w_dn': w_dn[l], 'b_dn': b_dn[l]}
        mk, mv = memory_kv(mem_prompt, g_mem[l], w_mk[l], w_mv[l])
        yp, c_new, g_new, s_new = decoder_layer(
            yp, mk, mv,
            jnp.zeros((nb, CONV_WIDTH - 1, CONV_CH), yp.dtype),
            jnp.zeros((nb, SHORT_CONV - 1, QKV_CH), yp.dtype),
            jnp.zeros((nb, GDN_HEADS, GDN_DK, GDN_DV), jnp.float32),
            p, True)
        pc.append(c_new)
        pg.append(g_new)
        ps.append(s_new.astype(x_prompt.dtype))
        pk.append(mk)
        pv.append(mv)
        ys, c2, g2, s2 = decoder_layer(
            ys, cache_mem_k[l], cache_mem_v[l], state_conformer_conv[l], state_gdn_conv[l],
            state_gdn[l].astype(jnp.float32), p, False)
        sc.append(c2.astype(state_conformer_conv.dtype))
        sg.append(g2.astype(state_gdn_conv.dtype))
        ss.append(s2.astype(state_gdn.dtype))
    y_prompt = rmsnorm(yp, g_final)
    y_sample = rmsnorm(ys, g_final)
    return (y_prompt, y_sample, jnp.stack(pc), jnp.stack(pg), jnp.stack(ps), jnp.stack(pk),
            jnp.stack(pv), jnp.stack(sc), jnp.stack(sg), jnp.stack(ss))


_drawn_inputs = setup_inputs


def setup_inputs(seed=0):
    import zlib

    import numpy as np

    out = dict(_drawn_inputs(seed))
    spreads = {}
    factors = {'g_xattn': 7.455, 'g_mem': 2.748, 'b_gu': 8.0, 'b_dn': 8.0, 'g_final': 2.782}
    for name, (base, spread) in spreads.items():
        noise = np.random.default_rng([zlib.crc32(name.encode()), seed]).standard_normal(out[name].shape)
        drawn = base * np.exp(spread * noise) if base else spread * noise
        out[name] = __import__('jax').numpy.asarray(drawn.astype(out[name].dtype))
    for name, factor in factors.items():
        out[name] = (out[name] * factor).astype(out[name].dtype)
    return out
```

```python
from contextlib import ExitStack

import concourse.bass as bass
from concourse import mybir

ALU = mybir.AluOpType
ACT = mybir.ActivationFunctionType
AX = mybir.AxisListType
F32 = mybir.dt.float32
I32 = mybir.dt.int32
U32 = mybir.dt.uint32
P = 128


def pre_moe_jobs(levels, sample_groups):
    jobs = [("param", 0), ("param", 1)]
    jobs += [("x_t", c) for c in range(8)]
    jobs += [("mix_norm",), ("short_hist",), ("ab",)]
    jobs += [("qkv", f) for f in range(12)]
    jobs += [("z", 0), ("decay_small",)]
    jobs += [("decay_row", 0), ("decay_row", 1), ("beta_row", 0), ("beta_row", 1)]
    jobs += [("l2", f) for f in (4, 5, 6, 7)] + [("z", 1)] + [("l2", f) for f in (0, 1, 2, 3)]
    jobs += [("v_tok", 0), ("v_tok", 1), ("z", 2), ("k_tok", 0), ("k_tok", 1)]
    jobs += [("kk", 0), ("kk", 1), ("z", 3), ("qk", 0), ("qk", 1)]
    jobs += [("inv_t", 0, 0), ("inv_t", 0, 1)]
    fill = [(n, i) for i in range(4) for n in ("glu_b", "glu_a")]
    for lv in range(1, levels):
        jobs += [("inv_x", lv, 0), ("inv_x", lv, 1)]
        jobs += [fill.pop(0)]
        jobs += [("inv_d", lv, 0), ("inv_d", lv, 1)]
        if lv < levels - 1:
            if lv in (2, 4) and fill:
                jobs += [fill.pop(0)]
            jobs += [("inv_t", lv, 0), ("inv_t", lv, 1)]
    jobs += fill
    jobs += [("w_neg",), ("v_new", 0), ("state", 0), ("v_new", 1), ("o_t", 0), ("o_t", 1), ("state", 1)]
    jobs += [("s_decay",), ("s_kq",), ("s_read",)] + [("s_outer", g) for g in range(sample_groups)]
    jobs += [("mem_t", c) for c in range(8)] + [("mem_norm",)]
    jobs += [("mk", t) for t in range(4)]
    jobs += [("o_norm", h) for h in range(4)]
    jobs += [("mv", t) for t in range(4)] + [("mk_t", j) for j in range(4)]
    jobs += [("conv_hist", j) for j in range(2)] + [("tail_g", j) for j in range(3)] + [("tail_c",)]
    jobs += [("ln_mean",), ("ln_var",)]
    jobs += [("w_out", d) for d in range(8)] + [("x_norm",)]
    jobs += [("xq", d) for d in range(8)] + [("q_s", 0), ("q_s", 1)]
    for t in range(2):
        jobs += [("score", t, 0), ("score", t, 1)]
    for t in range(2):
        jobs += [("prob_t", t, 0), ("prob_t", t, 1)]
    jobs += [("attn", d) for d in range(8)]
    jobs += [("s_score_t",), ("s_prob_t",), ("s_attn",)]
    jobs += [("xo", d) for d in range(8)] + [("moe_norm",)]
    jobs += [("logits",)] + [("h_tok", i) for i in range(6)] + [("position",), ("gate_t",)]
    jobs += [("b_dn", d) for d in range(8)]
    return jobs


def bass_hymba_step(nc, a, outs):
    (x_prompt, mem_prompt, x_sample, st_conf, st_short, st_gdn, cache_k, cache_v, w_in, b_glu, w_dw, b_dw,
     ln_g, ln_b, w_sc, a_log, dt_bias, g_onorm, w_out, g_mix, g_xattn, g_mem, w_xq, w_mk, w_mv, w_xo, g_moe,
     w_router, b_router, w_gu, b_gu, w_dn, b_dn, g_final) = a
    (y_prompt, y_sample, o_conf_p, o_short_p, o_gdn_p, o_mem_k, o_mem_v, o_conf_s, o_short_s, o_gdn_s) = outs

    TP = x_prompt.shape[1]
    TS = x_sample.shape[0]
    T = TP + TS
    D = x_prompt.shape[2]
    KT = D // P
    NT = TP // P
    H = st_gdn.shape[2]
    BH = TS * H
    E = w_gu.shape[1]
    TAPS = w_dw.shape[1]
    HC = TAPS - 1
    SC = w_sc.shape[1]
    HS = SC - 1
    QF = w_sc.shape[2] // P
    CF = w_dw.shape[2] // P
    NMEM = mem_prompt.shape[1]
    XH = cache_k.shape[3]
    XD = cache_k.shape[4]
    LEVELS = 7
    SLOTS = 64
    HALF = D // 2
    EPS = 1e-6
    GROUP = 4
    NG = BH // GROUP
    ROWS = [(0, 0, P), (1, P, P), (2, TP, TS)]

    with ExitStack() as ctx:
        def sb(name, shape, dt=F32):
            t = ctx.enter_context(nc.sbuf_tensor(name, shape, dt))
            return t[tuple(slice(None) for _ in shape)]

        sems = {}

        def sem(name):
            if name not in sems:
                sems[name] = ctx.enter_context(nc.semaphore(name))
            return sems[name]

        bank = [ctx.enter_context(nc.psum_tensor(f"bank{i}", [P, 512], F32)) for i in range(8)]
        JOB = {key: n for n, key in enumerate(pre_moe_jobs(LEVELS, NG))}
        N_PRE = len(JOB)
        TAIL = {key: n for n, key in enumerate([("fin_norm",)] + [("y_t", i) for i in range(6)])}

        def job(key):
            return (N_PRE + (-N_PRE) % 8 + TAIL[key]) if key in TAIL else JOB[key]

        def ps(key):
            return bank[job(key) % 8]

        def open_bank(pe, key):
            n = job(key)
            if key in TAIL:
                if TAIL[key] >= 8:
                    pe.wait_ge(sem(f"drained{n % 8}"), n // 8)
                return
            if n >= 8:
                pe.wait_ge(sem(f"drained{n % 8}"), n // 8)

        def uses(key):
            n = job(key)
            if key in TAIL:
                return sum(1 for m in range(N_PRE) if m % 8 == n % 8) + 1 + TAIL[key] // 8
            return n // 8 + 1

        def filled(ins, key):
            ins.then_inc(sem(f"filled{job(key) % 8}"), 1)

        def drained(ins, key):
            ins.then_inc(sem(f"drained{job(key) % 8}"), 1)

        def wait_filled(eng, *key):
            eng.wait_ge(sem(f"filled{job(key) % 8}"), uses(key))

        def wait_drained(eng, *key):
            eng.wait_ge(sem(f"drained{job(key) % 8}"), uses(key))

        ring = sb("ring", [P, 12, 2048])
        region_m = sb("region_m", [P, 8192])
        region_p = sb("region_p", [P, 10560])
        scratch = ring[:, 8:12, :].rearrange("p s n -> p (s n)")

        def carve(base, at, n, dims=None, **sizes):
            v = base[:, at:at + n]
            return v.rearrange(dims, **sizes) if dims else v

        ident = sb("ident", [P, P])
        tri = sb("tri", [P, P])
        tri_strict = sb("tri_strict", [P, P])
        ones = sb("ones", [P, P])
        iota = sb("iota", [P, 2 * SLOTS])
        par = sb("par", [P, 2, P])
        xT = sb("xT", [P, KT, T])
        hT = sb("hT", [P, KT, T])
        mix = sb("mix", [P, KT, T])
        rn = sb("rn", [P, 2, T])
        lnb = sb("lnb", [P, T])
        sig = sb("sig", [P, 2, T])
        wab = sb("wab", [P, KT, 2 * H])
        wr = sb("wr", [P, KT, E])
        br_bc = sb("br_bc", [P, E])
        small = sb("small", [P, 512])
        eps_t = sb("eps_t", [P, 4])

        x_tok = carve(region_m, 0, 3 * D, "p (t d) -> p t d", t=3)
        u_raw = carve(region_p, 0, QF * (HS + T), "p (f t) -> p f t", f=QF)
        qkv = carve(region_p, 3204, QF * T, "p (f t) -> p f t", f=QF)
        rows = carve(region_p, 3204, 2 * P, "p (a n) -> p a n", a=2)
        glu = carve(region_p, 6372, CF * (HC + T), "p (f t) -> p f t", f=CF)
        conv = carve(region_p, 7548, CF * T, "p (f t) -> p f t", f=CF)
        zg = carve(region_p, 8604, H * T, "p (f t) -> p f t", f=H)
        masks = carve(region_p, 9660, LEVELS * P, "p (l n) -> p l n", l=LEVELS)
        short_rows = scratch[0:TS * HS, 0:QF * P]
        short_hist = carve(scratch, 1536, QF * TS * HS, "p (f b j) -> p f b j", f=QF, b=TS)
        mix_sq = mix

        def tiles(base, at):
            return [carve(base, at + c * 512, 512, "p (h n) -> p h n", h=H) for c in range(NT)]

        decay, beta_row, neg_l, inv_x, inv_t = (tiles(scratch, 1024 * i) for i in range(5))
        k_bg, v_beta, k_dec, inv_u, intra, q_g = (tiles(region_m, 1024 * i) for i in range(6))
        v_new = tiles(region_m, 6144)
        w_neg = carve(region_m, 7168, 512, "p (h n) -> p h n", h=H)
        state = carve(region_m, 7680, 512, "p (h n) -> p h n", h=H)
        state_out = carve(scratch, 5120, 512, "p (h n) -> p h n", h=H)
        s_state = carve(scratch, 0, BH * P, "p (c n) -> p c n", c=BH)
        conv_rows = carve(scratch, 5632, 1024, "p (a n) -> p a n", a=2)
        conv_hist = carve(scratch, 6656, CF * TS * HC, "p (f b j) -> p f b j", f=CF, b=TS)
        tail_rows = carve(scratch, 7616, 512)
        memT = carve(region_m, 0, KT * NMEM, "p (c t) -> p c t", c=KT)
        mkT = carve(region_m, 2048, KT * NMEM, "p (c t) -> p c t", c=KT)
        mem_tok = carve(region_m, 4096, 2 * D, "p (t d) -> p t d", t=2)
        mk_tok = mem_tok
        mv_tok = carve(region_m, 6144, 2 * D, "p (t d) -> p t d", t=2)
        qT = carve(region_p, 0, KT * T, "p (c t) -> p c t", c=KT)
        oT = carve(region_p, 2112, KT * T, "p (c t) -> p c t", c=KT)
        probs = carve(region_p, 4224, 2048, "p (t h m) -> p t h m", t=NT, h=XH)
        pT = carve(region_p, 6272, 2048, "p (h u t) -> p h u t", h=XH, u=2)
        q_bc = carve(region_p, 8320, 2048, "p (s n) -> p s n", s=2)
        kv = [ring[:, 8 + i, :].rearrange("p (t d) -> p t d", t=2) for i in range(4)]
        s_sc = sb("s_sc", [P, 2, BH])
        s_pT = sb("s_pT", [P, 2, BH])
        s_pr = mix[0:BH, 0, 0:NMEM]
        q_s = mix[0:TS, 2:6, :].rearrange("p a b -> p (a b)")[:, 0:D]
        h_tok = carve(region_p, 0, 3 * D, "p (t d) -> p t d", t=3)
        y_out = carve(region_p, 0, 3 * D, "p (t d) -> p t d", t=3)
        lg = carve(region_p, 3072, 3 * (E + 4), "p (t e) -> p t e", t=3)
        lg_rep = carve(region_p, 3200, 3 * (E + 4), "p (t e) -> p t e", t=3)
        top8 = carve(region_p, 3328, 24, "p (t e) -> p t e", t=3)
        key8 = carve(region_p, 3360, 24, "p (t e) -> p t e", t=3)
        mask = carve(region_p, 3392, 3 * E, "p (t e) -> p t e", t=3)
        gate = carve(region_p, 3488, 3 * E, "p (t e) -> p t e", t=3)
        posm = carve(region_p, 3584, 3 * E, "p (t e) -> p t e", t=3)
        neg_top = carve(region_p, 3680, 4)
        gsum = carve(region_p, 3688, 4)
        cmax = carve(region_p, 3696, 8)
        gateT = carve(region_p, 3712, T)
        sel = carve(region_p, 4000, 3 * SLOTS, "p (t s) -> p t s", t=3)
        gsel = carve(region_p, 4192, 3 * P, "p (t s) -> p t s", t=3)
        scat = carve(region_p, 4576, T)
        one_hot = carve(region_p, 4840, SLOTS)
        hg_rows = carve(region_p, 4904, 512)
        xg = carve(region_p, 5416, 512)
        xl = carve(region_p, 5928, 512)
        sg = carve(region_p, 6440, 512)
        act_rows = carve(region_p, 6952, 512)
        y_rows = carve(region_p, 7464, 512)
        hg = carve(region_p, 7976, 512, "p (c m) -> p c m", c=4)
        act_t = carve(region_p, 8488, 512, "p (c m) -> p c m", c=4)
        b_gu_sb = carve(region_m, 2048, 2 * D)
        b_dn_sb = carve(region_m, 1024, D)
        n_items_i = sb("n_items_i", [P, 1], I32)

        q_scratch = nc.dram_tensor("q_scratch", (TS, D), F32, kind="Internal").ap()

        PR = {}
        at = 0
        for name, n in (("mix", 8), ("xattn", 8), ("mem", 8), ("moe", 8), ("final", 8), ("b_glu", 8),
                        ("b_dw", CF), ("ln_g", CF), ("ln_b", CF), ("onorm", 1), ("w_sc", SC * QF)):
            PR[name] = at
            at += n
        PAR_ROWS = at
        DW_ROWS = TAPS * CF

        def pcol(name, i):
            return par[:, 0, PR[name] + i:PR[name] + i + 1]

        def dw(tap, f):
            return par[:, 1, tap * CF + f:tap * CF + f + 1]

        ab = small[:, 0:24].rearrange("p (t n) -> p t n", t=3)
        dtb = small[:, 24:28]
        alog = small[:, 28:32]
        ealog = small[:, 32:36]
        tt_ = small[:, 36:48].rearrange("p (t n) -> p t n", t=3)
        ta = small[:, 48:60].rearrange("p (t n) -> p t n", t=3)
        g_log = small[:, 60:72].rearrange("p (t n) -> p t n", t=3)
        beta = small[:, 72:84].rearrange("p (t n) -> p t n", t=3)
        eb = small[:, 84:96].rearrange("p (t n) -> p t n", t=3)
        gs = small[:, 96:120]
        ge = small[:, 120:144]
        bg = small[:, 144:152]
        s_rhs = small[:, 160:224]
        s_eg = small[:, 224:256]
        s_beta = small[:, 256:288]
        s_kq = small[:, 288:320]
        s_r = small[:, 320:352]
        s_v = small[:, 352:384]
        s_o = small[:, 384:416]
        nmx = small[:, 416:424]
        ssum = small[:, 424:432]
        srec = small[:, 432:440]
        smx = small[:, 440:444]

        def cols(w, c0):
            return w[0, :, c0:c0 + 512].rearrange("(k p) n -> p k n", p=P)

        GROUPS = [("qkv", w_in, 1024), ("qkv", w_in, 1536), ("qkv", w_in, 2048), ("z", w_in, 2560),
                  ("glu_b", w_in, 512), ("glu_a", w_in, 0), ("mk", w_mk, 0), ("mk", w_mk, 512),
                  ("mv", w_mv, 0), ("mv", w_mv, 512), ("w_out", w_out, 0), ("w_out", w_out, 512),
                  ("xq", w_xq, 0), ("xq", w_xq, 512), ("xo", w_xo, 0), ("xo", w_xo, 512)]
        LAST = [("qkv", 3), ("qkv", 7), ("qkv", 11), ("z", 3), ("glu_b", 3), ("glu_a", 3), ("mk", 1), ("mk", 3),
                ("mv", 1), ("mv", 3), ("w_out", 3), ("w_out", 7), ("xq", 3), ("xq", 7), ("xo", 3), ("xo", 7)]

        def wslot(g):
            return ring[:, 2 * (g % 4):2 * (g % 4) + 2, :].rearrange("p s n -> p (s n)").rearrange(
                "p (k n) -> p k n", k=KT)

        block = ctx.enter_context(nc.Block())

        def gu_piece(e, k):
            return w_gu[0, e, k * P:(k + 1) * P, :]

        def dn_piece(e, j):
            return w_dn[0, e, 2 * j * P:2 * (j + 1) * P, :].rearrange("(t p) n -> p t n", p=P)

        @block.sync
        def _(sp):
            for g, (_, w, c0) in enumerate(GROUPS):
                if g >= 4:
                    wait_filled(sp, *LAST[g - 4])
                sp.dma_start(wslot(g), cols(w, c0)).then_inc(sem(f"group{g % 4}"), 16)
                if g == 8:
                    wait_drained(sp, "inv_d", LEVELS - 1, 1)
                    sp.dma_start(s_state, st_gdn[0].rearrange("b h k v -> k (b h) v")).then_inc(sem("s_state_in"), 16)
                    wait_drained(sp, "state", 1)
                    wait_drained(sp, "o_t", 1)
                    sp.dma_start(mem_tok, mem_prompt[0].rearrange("(t p) d -> p t d", p=P)).then_inc(sem("mem_in"), 16)
            sp.wait_ge(sem("s_state_out"), 16)
            sp.wait_ge(sem("tails_out"), 16 * 8)
            sp.wait_ge(sem("conv_done"), CF)
            sp.wait_ge(sem("state_p_out"), 16)
            for i in range(2 * TS):
                if i >= 4:
                    j = i - 4
                    if j < TS:
                        sp.wait_ge(sem("k_used"), j + 1)
                    else:
                        sp.wait_ge(sem("v_used"), j - TS + 1)
                src = (cache_k if i < TS else cache_v)[0, i % TS].rearrange("(t p) h d -> p t (h d)", p=P)
                sp.dma_start(kv[i % 4], src).then_inc(sem(f"kv{i % 4}"), 16)
            for s in (0, 1, 2, 3, 8, 9, 10, 11, 4, 5, 6, 7):
                if s < 8:
                    wait_filled(sp, *LAST[12 + s // 2])
                elif s == 8:
                    wait_filled(sp, "s_attn")
                src = gu_piece(0, s) if s < 8 else dn_piece(0, s - 8)
                dst = ring[:, s, :] if s < 8 else ring[:, s, :].rearrange("p (t n) -> p t n", t=2)
                sp.dma_start(dst, src).then_inc(sem(f"piece{s}"), 16)
            sp.wait_ge(sem("routed"), 1)
            n = sp.value_load(n_items_i[0:1, 0:1], min_val=E, max_val=5 * E)
            with sp.Fori(1, n) as i:
                e = i % E
                for s in range(12):
                    sp.wait_ge(sem("piece_used"), 12 * i + (s - 11))
                    src = gu_piece(e, s) if s < 8 else dn_piece(e, s - 8)
                    dst = ring[:, s, :] if s < 8 else ring[:, s, :].rearrange("p (t n) -> p t n", t=2)
                    sp.dma_start(dst, src).then_inc(sem(f"piece{s}"), 16)

        @block.gpsimd
        def _(pool):
            pool.memset(ident[:, :], 0.0)
            pool.memset(ones[:, :], 1.0)
            pool.memset(tri[:, :], 1.0)
            pool.memset(tri_strict[:, :], 1.0)
            pool.memset(masks, 0.0)
            pool.memset(eps_t[:, 0:1], EPS)
            pool.memset(eps_t[:, 1:2], -0.5 * float(_log(P)))
            pool.memset(eps_t[:, 2:3], 1.0)
            pool.iota(iota[:, :], [[0, 2], [1, SLOTS]], 0, 0, allow_small_or_imprecise_dtypes=True).then_inc(sem("const0"), 1)
            pool.wait_ge(sem("const0"), 1)
            pool.affine_select(out=ident[:, :], in_=ident[:, :], compare_op=ALU.not_equal, fill=1.0, base=0,
                               pattern=[[-1, P]], channel_multiplier=1)
            pool.affine_select(out=tri[:, :], in_=tri[:, :], compare_op=ALU.is_ge, fill=0.0, base=0,
                               pattern=[[1, P]], channel_multiplier=-1)
            pool.affine_select(out=tri_strict[:, :], in_=tri_strict[:, :], compare_op=ALU.is_gt, fill=0.0, base=0,
                               pattern=[[1, P]], channel_multiplier=-1).then_inc(sem("const"), 1)
            for lv in range(LEVELS):
                s = 1 << lv
                v = masks[:, lv, :].rearrange("p (b u r) -> p b u r", u=2, r=s)[:, :, 1, :]
                pool.memset(v, 1.0).then_inc(sem("masks"), 1)
                pool.wait_ge(sem("masks"), 3 * lv + 1)
                pool.affine_select(out=v, in_=v, compare_op=ALU.is_ge, fill=0.0, base=0,
                                   pattern=[[-2 * s, P // (2 * s)], [0, s]], channel_multiplier=1).then_inc(
                    sem("masks"), 1)
                pool.wait_ge(sem("masks"), 3 * lv + 2)
                pool.affine_select(out=v, in_=v, compare_op=ALU.is_ge, fill=0.0, base=s - 1,
                                   pattern=[[2 * s, P // (2 * s)], [0, s]], channel_multiplier=-1).then_inc(
                    sem("masks"), 1)
            pool.dma_start(o_conf_s[0, :, 0:HC - 1, :], st_conf[0, :, 1:HC, :]).then_inc(sem("stores"), 16)
            pool.dma_start(o_short_s[0, :, 0:HS - 1, :], st_short[0, :, 1:HS, :]).then_inc(sem("stores"), 16)
            wait_drained(pool, "inv_d", LEVELS - 1, 1)
            pool.dma_start(conv_rows[0:120, :, :], st_conf[0].rearrange("b j c -> (b j) c").rearrange(
                "(a p) c -> p a c", a=2)).then_inc(sem("conv_rows_in"), 16)
            wait_drained(pool, "state", 1)
            pool.dma_start(o_gdn_p[0, 0].rearrange("h k v -> k h v"), state_out).then_inc(sem("state_p_out"), 16)
            for g in range(NG):
                wait_drained(pool, "s_outer", g)
            pool.dma_start(o_gdn_s[0].rearrange("b h k v -> k (b h) v"), s_state).then_inc(sem("s_state_out"), 16)
            for t in range(2):
                for hf in range(2):
                    wait_drained(pool, "mk", 2 * hf + t)
            pool.dma_start(o_mem_k[0, 0].rearrange("(t p) h d -> p t (h d)", p=P), mk_tok).then_inc(sem("mk_out"), 16)
            for t in range(4):
                wait_drained(pool, "mv", t)
            pool.dma_start(o_mem_v[0, 0].rearrange("(t p) h d -> p t (h d)", p=P), mv_tok).then_inc(sem("mv_out"), 16)
            for j in range(3):
                wait_drained(pool, "tail_g", j)
                c0 = j * 512
                pool.dma_start(o_short_p[0, 0, :, c0:c0 + 512], tail_rows[0:HS, :]).then_inc(sem("tails_out"), 16)
                pool.dma_start(o_short_s[0, :, HS - 1, c0:c0 + 512], tail_rows[HS:HS + TS, :]).then_inc(
                    sem("tails_out"), 16)
            wait_drained(pool, "tail_c")
            pool.dma_start(o_conf_p[0, 0], tail_rows[0:HC, :]).then_inc(sem("tails_out"), 16)
            pool.dma_start(o_conf_s[0, :, HC - 1, :], tail_rows[HC:HC + TS, :]).then_inc(sem("tails_out"), 16)
            wait_drained(pool, "q_s", 0)
            wait_drained(pool, "q_s", 1)
            pool.dma_start(q_scratch, q_s).then_inc(sem("q_scratch"), 16)
            pool.wait_ge(sem("q_scratch"), 16)
            for b in range(TS):
                if b >= 2:
                    pool.wait_ge(sem("k_used"), b - 1)
                pool.dma_start(q_bc[:, b % 2, :], q_scratch[b:b + 1, :].to_broadcast([P, D])).then_inc(
                    sem(f"q_bc{b % 2}"), 16)
            for d in range(8):
                wait_drained(pool, "attn", d)
            pool.wait_ge(sem("mk_out"), 16)
            pool.wait_ge(sem("mv_out"), 16)
            pool.memset(b_gu_sb, 0.0).then_inc(sem("b_gu_zero"), 1)
            pool.wait_ge(sem("b_gu_zero"), 1)
            pool.dma_start(b_gu_sb[0:E, :], b_gu[0]).then_inc(sem("b_gu_in"), 16)
            pool.dma_start(b_dn_sb[0:E, :], b_dn[0]).then_inc(sem("b_dn_in"), 16)
            pool.wait_ge(sem("stores"), 32)
            for t, r0, m in ROWS:
                wait_drained(pool, "y_t", 2 * t)
                wait_drained(pool, "y_t", 2 * t + 1)
                dst = y_prompt[0, r0:r0 + P, :] if t < 2 else y_sample[:, 0, :]
                pool.dma_start(dst, y_out[0:m, t, :]).then_inc(sem("stores"), 16)
            pool.wait_ge(sem("stores"), 16 * 5)

        @block.tensor
        def _(pe):
            def project(key, g, f, src, width):
                open_bank(pe, key)
                pe.wait_ge(sem(f"group{g % 4}"), 16 * (g // 4 + 1))
                w = wslot(g)
                for k in range(KT):
                    m = pe.matmul(ps(key)[:, 0:width], w[:, k, f * P:(f + 1) * P], src[:, k, 0:width],
                                  start=(k == 0), stop=(k == KT - 1))
                filled(m, key)

            def column_sums(key, sq, n, width):
                open_bank(pe, key)
                for k in range(n):
                    m = pe.matmul(ps(key)[:, 0:width], ones[:, :], sq[:, k, 0:width], start=(k == 0), stop=(k == n - 1))
                filled(m, key)

            for key in sorted(JOB, key=JOB.get):
                kind = key[0]
                if kind == "param":
                    if key[1] == 0:
                        pe.wait_ge(sem("const"), 1)
                        pe.wait_ge(sem("param_in"), 16 * 12)
                    n = PAR_ROWS if key[1] == 0 else DW_ROWS
                    open_bank(pe, key)
                    filled(pe.transpose(ps(key)[:, 0:n], rows[0:n, key[1], :], ident[0:n, 0:n]), key)
                elif kind == "x_t":
                    c = key[1]
                    if c == 0:
                        pe.wait_ge(sem("x_in"), 32)
                    open_bank(pe, key)
                    for t, r0, m in ROWS:
                        ins = pe.transpose(ps(key)[:, r0:r0 + m], x_tok[0:m, t, c * P:(c + 1) * P], ident[0:m, 0:m])
                    filled(ins, key)
                elif kind == "mix_norm":
                    pe.wait_ge(sem("x_sq"), KT)
                    column_sums(key, mix_sq, KT, T)
                elif kind == "short_hist":
                    open_bank(pe, key)
                    pe.wait_ge(sem("short_in"), 16)
                    n = TS * HS
                    for f in range(QF):
                        ins = pe.transpose(ps(key)[:, f * n:(f + 1) * n], short_rows[:, f * P:(f + 1) * P],
                                           ident[0:n, 0:n])
                    filled(ins, key)
                elif kind == "ab":
                    open_bank(pe, key)
                    pe.wait_ge(sem("h_mix"), KT)
                    pe.wait_ge(sem("wab_in"), 16)
                    for t, r0, m in ROWS:
                        for k in range(KT):
                            ins = pe.matmul(ps(key)[0:m, 8 * t:8 * t + 8], hT[:, k, r0:r0 + m], wab[:, k, :],
                                            start=(k == 0), stop=(k == KT - 1))
                    filled(ins, key)
                elif kind == "qkv":
                    project(key, key[1] // 4, key[1] % 4, hT, T)
                elif kind == "z":
                    project(key, 3, key[1], hT, T)
                elif kind == "glu_b":
                    project(key, 4, key[1], hT, T)
                elif kind == "glu_a":
                    project(key, 5, key[1], hT, T)
                elif kind == "decay_small":
                    open_bank(pe, key)
                    pe.wait_ge(sem("g_log"), 1)
                    for c in range(NT):
                        pe.matmul(ps(key)[:, 4 * c:4 * c + 4], tri[:, :], g_log[:, c, :], start=True, stop=True)
                    for c in range(NT):
                        ins = pe.matmul(ps(key)[:, 8 + 4 * c:12 + 4 * c], ones[:, :], g_log[:, c, :], start=True,
                                        stop=True)
                    filled(ins, key)
                elif kind in ("decay_row", "beta_row"):
                    c = key[1]
                    src = (inv_x if kind == "decay_row" else inv_t)[c]
                    open_bank(pe, key)
                    pe.wait_ge(sem(kind), c + 1)
                    filled(pe.matmul(ps(key)[:, :], ones[:, :], src.rearrange("p h n -> p (h n)"), start=True,
                                     stop=True), key)
                elif kind == "l2":
                    f = key[1]
                    open_bank(pe, key)
                    pe.wait_ge(sem("qk_sq"), f + 1)
                    filled(pe.matmul(ps(key)[:, 0:T], ones[:, :], mix_sq[:, f, :], start=True, stop=True), key)
                elif kind in ("v_tok", "k_tok"):
                    c = key[1]
                    open_bank(pe, key)
                    if kind == "v_tok":
                        pe.wait_ge(sem("qkv_silu"), QF)
                    else:
                        pe.wait_ge(sem("unit"), H)
                    f0 = 2 * H if kind == "v_tok" else H
                    for h in range(H):
                        ins = pe.transpose(ps(key)[:, h * P:(h + 1) * P], qkv[:, f0 + h, c * P:(c + 1) * P],
                                           ident[:, :])
                    filled(ins, key)
                elif kind in ("kk", "qk"):
                    c = key[1]
                    open_bank(pe, key)
                    if kind == "qk":
                        pe.wait_ge(sem("unit"), 2 * H)
                    for h in range(H):
                        k_c = qkv[:, H + h, c * P:(c + 1) * P]
                        r = k_c if kind == "kk" else qkv[:, h, c * P:(c + 1) * P]
                        ins = pe.matmul(ps(key)[:, h * P:(h + 1) * P], k_c, r, start=True, stop=True)
                    filled(ins, key)
                elif kind == "inv_t":
                    lv, c = key[1:]
                    open_bank(pe, key)
                    if lv == 0:
                        pe.wait_ge(sem("inv_start"), c + 1)
                    else:
                        wait_drained(pe, "inv_d", lv, c)
                    for h in range(H):
                        ins = pe.transpose(ps(key)[:, h * P:(h + 1) * P], inv_u[c][:, h, :], ident[:, :])
                    filled(ins, key)
                elif kind == "inv_x":
                    lv, c = key[1:]
                    open_bank(pe, key)
                    wait_drained(pe, "inv_t", lv - 1, c)
                    for h in range(H):
                        ins = pe.matmul(ps(key)[:, h * P:(h + 1) * P], neg_l[c][:, h, :], inv_t[c][:, h, :],
                                        start=True, stop=True)
                    filled(ins, key)
                elif kind == "inv_d":
                    lv, c = key[1:]
                    open_bank(pe, key)
                    wait_drained(pe, "inv_x", lv, c)
                    for h in range(H):
                        ins = pe.matmul(ps(key)[:, h * P:(h + 1) * P], inv_x[c][:, h, :], inv_u[c][:, h, :],
                                        start=True, stop=True)
                    filled(ins, key)
                elif kind == "w_neg":
                    open_bank(pe, key)
                    wait_drained(pe, "inv_d", LEVELS - 1, 0)
                    wait_drained(pe, "inv_d", LEVELS - 1, 1)
                    wait_drained(pe, "k_tok", 1)
                    for h in range(H):
                        ins = pe.matmul(ps(key)[:, h * P:(h + 1) * P], k_bg[1][:, h, :], inv_u[1][:, h, :],
                                        start=True, stop=True)
                    filled(ins, key)
                elif kind == "v_new":
                    c = key[1]
                    open_bank(pe, key)
                    wait_drained(pe, "v_tok", c)
                    if c:
                        wait_drained(pe, "w_neg")
                        wait_drained(pe, "state", 0)
                    for h in range(H):
                        o = ps(key)[:, h * P:(h + 1) * P]
                        ins = pe.matmul(o, inv_u[c][:, h, :], v_beta[c][:, h, :], start=True, stop=(c == 0))
                        if c:
                            ins = pe.matmul(o, w_neg[:, h, :], state[:, h, :], start=False, stop=True)
                    filled(ins, key)
                elif kind == "state":
                    c = key[1]
                    open_bank(pe, key)
                    wait_drained(pe, "v_new", c)
                    wait_drained(pe, "k_tok", c)
                    for h in range(H):
                        ins = pe.matmul(ps(key)[:, h * P:(h + 1) * P], k_dec[c][:, h, :], v_new[c][:, h, :],
                                        start=True, stop=True)
                    filled(ins, key)
                elif kind == "o_t":
                    c = key[1]
                    open_bank(pe, key)
                    wait_drained(pe, "v_new", c)
                    wait_drained(pe, "qk", c)
                    for h in range(H):
                        o = ps(key)[:, h * P:(h + 1) * P]
                        ins = pe.matmul(o, v_new[c][:, h, :], intra[c][:, h, :], start=True, stop=(c == 0))
                        if c:
                            pe.wait_ge(sem("q_g"), 1)
                            ins = pe.matmul(o, state[:, h, :], q_g[1][:, h, :], start=False, stop=True)
                    filled(ins, key)
                elif kind == "s_decay":
                    open_bank(pe, key)
                    pe.wait_ge(sem("s_rhs"), 1)
                    filled(pe.matmul(ps(key)[:, 0:2 * BH], ones[0:TS, :], s_rhs[0:TS, :], start=True, stop=True), key)
                elif kind == "s_kq":
                    open_bank(pe, key)
                    pe.wait_ge(sem("s_kq"), 1)
                    filled(pe.matmul(ps(key)[:, 0:BH], ones[:, :], s_kq[:, :], start=True, stop=True), key)
                elif kind == "s_read":
                    open_bank(pe, key)
                    pe.wait_ge(sem("s_state_in"), 16)
                    for b in range(TS):
                        for h in range(H):
                            c = b * H + h
                            ins = pe.matmul(ps(key)[:, 2 * c:2 * c + 2], s_state[:, c, :],
                                            qkv[:, h:h + H + 1:H, TP + b], start=True, stop=True)
                    filled(ins, key)
                elif kind == "s_outer":
                    open_bank(pe, key)
                    if key[1] == 0:
                        pe.wait_ge(sem("s_vn"), 1)
                    for j in range(GROUP):
                        c = key[1] * GROUP + j
                        ins = pe.matmul(ps(key)[:, j * P:(j + 1) * P], s_v[:, c:c + 1].to_broadcast([P, P]),
                                        ident[:, :], start=True, stop=True)
                    filled(ins, key)
                elif kind == "mem_t":
                    open_bank(pe, key)
                    if key[1] == 0:
                        pe.wait_ge(sem("mem_in"), 16)
                    for t in range(2):
                        ins = pe.transpose(ps(key)[:, t * P:(t + 1) * P], mem_tok[:, t, key[1] * P:(key[1] + 1) * P],
                                           ident[:, :])
                    filled(ins, key)
                elif kind == "mem_norm":
                    pe.wait_ge(sem("mem_sq"), KT)
                    column_sums(key, mkT, KT, NMEM)
                elif kind in ("mk", "mv"):
                    g = (6 if kind == "mk" else 8) + key[1] // 2
                    t = key[1] % 2
                    open_bank(pe, key)
                    pe.wait_ge(sem("mem_h"), KT)
                    pe.wait_ge(sem(f"group{g % 4}"), 16 * (g // 4 + 1))
                    for k in range(KT):
                        ins = pe.matmul(ps(key)[:, :], memT[:, k, t * P:(t + 1) * P], wslot(g)[:, k, :],
                                        start=(k == 0), stop=(k == KT - 1))
                    filled(ins, key)
                elif kind == "mk_t":
                    open_bank(pe, key)
                    for t in range(4):
                        wait_drained(pe, "mk", t)
                    for u in range(2):
                        for t in range(2):
                            ct = 2 * key[1] + u
                            ins = pe.transpose(ps(key)[:, (2 * u + t) * P:(2 * u + t + 1) * P],
                                               mk_tok[:, t, ct * P:(ct + 1) * P], ident[:, :])
                    filled(ins, key)
                elif kind == "o_norm":
                    h = key[1]
                    open_bank(pe, key)
                    pe.wait_ge(sem("o_sq"), h + 1)
                    filled(pe.matmul(ps(key)[:, 0:T], ones[:, :], mix[:, h, :], start=True, stop=True), key)
                elif kind == "conv_hist":
                    open_bank(pe, key)
                    pe.wait_ge(sem("conv_rows_in"), 16)
                    for u in range(2):
                        f = 2 * key[1] + u
                        for a2 in range(2):
                            c0 = (2 * u + a2) * 120
                            ins = pe.transpose(ps(key)[:, c0:c0 + 120], conv_rows[0:120, a2, f * P:(f + 1) * P],
                                               ident[0:120, 0:120])
                    filled(ins, key)
                elif kind == "tail_g":
                    open_bank(pe, key)
                    for u in range(4):
                        ins = pe.transpose(ps(key)[0:HS + TS, u * P:(u + 1) * P],
                                           u_raw[:, 4 * key[1] + u, TP:TP + HS + TS], ident[:, :])
                    filled(ins, key)
                elif kind == "tail_c":
                    open_bank(pe, key)
                    for i in range(4):
                        wait_drained(pe, "glu_a", i)
                    for f in range(CF):
                        ins = pe.transpose(ps(key)[0:HC + TS, f * P:(f + 1) * P], glu[:, f, TP:TP + HC + TS],
                                           ident[:, :])
                    filled(ins, key)
                elif kind == "ln_mean":
                    pe.wait_ge(sem("conv_done"), CF)
                    column_sums(key, conv, CF, T)
                elif kind == "ln_var":
                    pe.wait_ge(sem("ln_sq"), 1)
                    column_sums(key, glu, CF, T)
                elif kind == "w_out":
                    if key[1] == 0:
                        pe.wait_ge(sem("mix_conv"), CF)
                        pe.wait_ge(sem("mix_gdn"), 1)
                    project(key, 10 + key[1] // 4, key[1] % 4, mix, T)
                elif kind == "x_norm":
                    pe.wait_ge(sem("x2_sq"), KT)
                    column_sums(key, mix_sq, KT, T)
                elif kind == "xq":
                    if key[1] == 0:
                        pe.wait_ge(sem("h_xattn"), KT)
                    project(key, 12 + key[1] // 4, key[1] % 4, hT, T)
                elif kind == "q_s":
                    open_bank(pe, key)
                    for u in range(4):
                        d = 4 * key[1] + u
                        wait_drained(pe, "xq", d)
                        ins = pe.transpose(ps(key)[0:TS, u * P:(u + 1) * P], qT[:, d, TP:T], ident[:, :])
                    filled(ins, key)
                elif kind == "score":
                    t, hp = key[1:]
                    open_bank(pe, key)
                    for j in range(4):
                        wait_drained(pe, "mk_t", j)
                    for u in range(2):
                        h = 2 * hp + u
                        for dd in range(2):
                            ins = pe.matmul(ps(key)[:, u * NMEM:(u + 1) * NMEM], qT[:, 2 * h + dd, t * P:(t + 1) * P],
                                            mkT[:, 2 * h + dd, :], start=(dd == 0), stop=(dd == 1))
                    filled(ins, key)
                elif kind == "prob_t":
                    t, hp = key[1:]
                    open_bank(pe, key)
                    pe.wait_ge(sem("probs"), 4 * t + 2 * hp + 2)
                    for u in range(2):
                        for m in range(2):
                            ins = pe.transpose(ps(key)[:, (2 * u + m) * P:(2 * u + m + 1) * P],
                                               probs[:, t, 2 * hp + u, m * P:(m + 1) * P], ident[:, :])
                    filled(ins, key)
                elif kind == "attn":
                    d = key[1]
                    h = d // 2
                    open_bank(pe, key)
                    for t in range(2):
                        wait_drained(pe, "prob_t", t, h // 2)
                    for j in range(4):
                        wait_drained(pe, "mv", j)
                    for m in range(2):
                        ins = pe.matmul(ps(key)[:, 0:TP], mv_tok[:, m, d * P:(d + 1) * P], pT[:, h, m, :],
                                        start=(m == 0), stop=(m == 1))
                    filled(ins, key)
                elif kind == "s_score_t":
                    open_bank(pe, key)
                    pe.wait_ge(sem("k_used"), TS)
                    for m in range(2):
                        ins = pe.transpose(ps(key)[0:BH, m * P:(m + 1) * P], s_sc[:, m, :], ident[:, :])
                    filled(ins, key)
                elif kind == "s_prob_t":
                    open_bank(pe, key)
                    pe.wait_ge(sem("s_probs"), 1)
                    for m in range(2):
                        ins = pe.transpose(ps(key)[:, m * BH:(m + 1) * BH], s_pr[:, m * P:(m + 1) * P],
                                           ident[0:BH, 0:BH])
                    filled(ins, key)
                elif kind == "s_attn":
                    open_bank(pe, key)
                    wait_drained(pe, "s_prob_t")
                    for b in range(TS):
                        i = TS + b
                        pe.wait_ge(sem(f"kv{i % 4}"), 16 * (i // 4 + 1))
                        for d in range(8):
                            for m in range(2):
                                c = b * XH + d // 2
                                ins = pe.matmul(ps(key)[:, d * TS + b:d * TS + b + 1], kv[i % 4][:, m, d * P:(d + 1) * P],
                                                s_pT[:, m, c:c + 1], start=(m == 0), stop=(m == 1))
                        if b < TS - 1:
                            ins.then_inc(sem("v_used"), 1)
                        else:
                            filled(ins, key)
                elif kind == "xo":
                    if key[1] == 0:
                        for d in range(8):
                            wait_drained(pe, "attn", d)
                        wait_drained(pe, "s_attn")
                    project(key, 14 + key[1] // 4, key[1] % 4, oT, T)
                elif kind == "moe_norm":
                    pe.wait_ge(sem("x3_sq"), KT)
                    column_sums(key, mix_sq, KT, T)
                elif kind == "logits":
                    open_bank(pe, key)
                    pe.wait_ge(sem("h_moe"), KT)
                    pe.wait_ge(sem("wr_in"), 32)
                    for t, r0, m in ROWS:
                        for k in range(KT):
                            ins = pe.matmul(ps(key)[0:m, E * t:E * t + E], hT[:, k, r0:r0 + m], wr[:, k, :],
                                            start=(k == 0), stop=(k == KT - 1))
                    filled(ins, key)
                elif kind == "h_tok":
                    t, hf = divmod(key[1], 2)
                    _, r0, m = ROWS[t]
                    open_bank(pe, key)
                    for u in range(4):
                        ins = pe.transpose(ps(key)[0:m, u * P:(u + 1) * P], hT[:, 4 * hf + u, r0:r0 + m], ident[:, :])
                    filled(ins, key)
                elif kind == "position":
                    open_bank(pe, key)
                    pe.wait_ge(sem("mask"), 1)
                    o = ps(key)
                    pe.matmul(o[:, 0:E], tri_strict[:, :], mask[:, 0, :], start=True, stop=True)
                    pe.matmul(o[:, E:2 * E], ones[:, :], mask[:, 0, :], start=True, stop=False)
                    pe.matmul(o[:, E:2 * E], tri_strict[:, :], mask[:, 1, :], start=False, stop=True)
                    pe.matmul(o[:, 2 * E:3 * E], ones[:, :], mask[:, 0, :], start=True, stop=False)
                    pe.matmul(o[:, 2 * E:3 * E], ones[:, :], mask[:, 1, :], start=False, stop=False)
                    pe.matmul(o[:, 2 * E:3 * E], tri_strict[0:TS, :], mask[0:TS, 2, :], start=False, stop=True)
                    pe.matmul(o[:, 3 * E:4 * E], ones[:, :], mask[:, 0, :], start=True, stop=False)
                    pe.matmul(o[:, 3 * E:4 * E], ones[:, :], mask[:, 1, :], start=False, stop=False)
                    filled(pe.matmul(o[:, 3 * E:4 * E], ones[0:TS, :], mask[0:TS, 2, :], start=False, stop=True), key)
                elif kind == "gate_t":
                    open_bank(pe, key)
                    pe.wait_ge(sem("gate"), 3)
                    for t, r0, m in ROWS:
                        ins = pe.transpose(ps(key)[0:E, r0:r0 + m], gate[0:m, t, :], ident[0:m, 0:m])
                    filled(ins, key)
                elif kind == "b_dn":
                    open_bank(pe, key)
                    if key[1] == 0:
                        pe.wait_ge(sem("b_dn_in"), 16)
                        wait_drained(pe, "gate_t")
                    d = key[1]
                    filled(pe.matmul(ps(key)[:, 0:T], b_dn_sb[0:E, d * P:(d + 1) * P], gateT[0:E, :], start=True,
                                     stop=True), key)

            for n in range(max(0, N_PRE - 8), N_PRE):
                pe.wait_ge(sem(f"drained{n % 8}"), n // 8 + 1)
            pe.wait_ge(sem("routed"), 1)
            n_items = pe.value_load(n_items_i[0:1, 0:1], min_val=E, max_val=5 * E)

            def halves(n, lhs, rhs0, rhs1, start, stop):
                for u, rhs in ((0, rhs0), (1, rhs1)):
                    ins = pe.matmul(bank[n][u * SLOTS:(u + 1) * SLOTS, :], lhs, rhs, start=start, stop=stop)
                return ins

            def gather(i):
                pe.wait_ge(sem("sel_ready"), i + 1)
                pe.wait_ge(sem("hg_rows_ready"), i + 1)
                for t, r0, m in ROWS:
                    ins = halves(2, sel[0:m, t, :], h_tok[0:m, t, 0:512], h_tok[0:m, t, 512:1024], t == 0, t == 2)
                ins.then_inc(sem("gathered"), 1)

            def turn(n, dst_bank, s):
                for c in range(4):
                    ins = pe.transpose(bank[dst_bank][:, c * P:(c + 1) * P], n[:, c * P:(c + 1) * P], ident[:, :])
                ins.then_inc(sem(s), 1)

            def turn_gathered(i):
                pe.wait_ge(sem("hg_rows_ready"), i + 2)
                pe.wait_ge(sem("hg_ready"), i + 1)
                turn(hg_rows, 3, "hg_t")

            def scatter(i):
                pe.wait_ge(sem("gsel_ready"), i + 1)
                pe.wait_ge(sem("scat_added"), 8 * i + 1)
                for t, r0, m in ROWS:
                    ins = pe.transpose(bank[6][:, r0:r0 + m], gsel[0:m, t, :], ident[0:m, 0:m])
                ins.then_inc(sem("scat_t"), 1)
                pe.wait_ge(sem("scat_sb"), i + 1)
                pe.wait_ge(sem("y_ready"), i + 1)
                for n in range(8):
                    u, c = n % 2, n // 2
                    if n >= 2:
                        pe.wait_ge(sem("scat_added"), 8 * i + n)
                    pe.matmul(bank[7 - u][:, 0:T], y_rows[u * SLOTS:(u + 1) * SLOTS, c * P:(c + 1) * P],
                              scat[u * SLOTS:(u + 1) * SLOTS, :], start=True, stop=True).then_inc(
                        sem("scattered"), 1)

            gather(0)
            turn_gathered(0)
            with pe.Fori(0, n_items) as i:
                pe.wait_ge(sem("one_hot"), i + 1)
                pe.wait_ge(sem("gu_read"), i + 1)
                for n in range(2):
                    halves(n, one_hot, b_gu_sb[:, n * D:n * D + 512], b_gu_sb[:, n * D + 512:n * D + 1024], True, False)
                pe.wait_ge(sem("hg_ready"), i + 2)
                for k in range(8):
                    pe.wait_ge(sem(f"piece{k}"), 16 * i + 16)
                    x_k = hg[:, k % 4, (k // 4) * SLOTS:(k // 4 + 1) * SLOTS]
                    for n in range(2):
                        ins = halves(n, x_k, ring[:, k, n * D:n * D + 512], ring[:, k, n * D + 512:n * D + 1024],
                                     False, k == 7)
                    ins.then_inc(sem("piece_used"), 1)
                scatter(i)
                gather(i + 1)
                pe.wait_ge(sem("act_ready"), i + 1)
                turn(act_rows, 4, "act_turned")
                turn_gathered(i + 1)
                pe.wait_ge(sem("act_t_ready"), i + 1)
                for j in range(4):
                    pe.wait_ge(sem(f"piece{8 + j}"), 16 * i + 16)
                    for v in range(2):
                        f = 2 * j + v
                        w = ring[:, 8 + j, v * D:(v + 1) * D]
                        ins = halves(5, act_t[:, f % 4, (f // 4) * SLOTS:(f // 4 + 1) * SLOTS], w[:, 0:512],
                                     w[:, 512:1024], f == 0, f == 7)
                    ins.then_inc(sem("piece_used"), 1)
            scatter(n_items)

            open_bank(pe, ("fin_norm",))
            pe.wait_ge(sem("hg_ready"), n_items + 2)
            pe.wait_ge(sem("x4_sq"), KT)
            column_sums(("fin_norm",), mix_sq, KT, T)
            for i in range(6):
                key = ("y_t", i)
                t, hf = divmod(i, 2)
                _, r0, m = ROWS[t]
                open_bank(pe, key)
                pe.wait_ge(sem("h_fin"), KT)
                for u in range(4):
                    ins = pe.transpose(ps(key)[0:m, u * P:(u + 1) * P], hT[:, 4 * hf + u, r0:r0 + m], ident[:, :])
                filled(ins, key)

        @block.scalar
        def _(act):
            def load(dst, src, s):
                act.dma_start(dst, src).then_inc(sem(s), 16)

            load(x_tok[:, 0:2, :], x_prompt[0].rearrange("(t p) d -> p t d", p=P), "x_in")
            load(x_tok[0:TS, 2, :], x_sample[:, 0, :], "x_in")
            for name, w, n in (("mix", g_mix, 8), ("xattn", g_xattn, 8), ("mem", g_mem, 8), ("moe", g_moe, 8),
                               ("b_glu", b_glu, 8), ("b_dw", b_dw, CF), ("ln_g", ln_g, CF), ("ln_b", ln_b, CF),
                               ("onorm", g_onorm, 1)):
                load(rows[PR[name]:PR[name] + n, 0, :], w[0].rearrange("(c p) -> c p", p=P), "param_in")
            load(rows[PR["final"]:PR["final"] + 8, 0, :], g_final.rearrange("(c p) -> c p", p=P), "param_in")
            load(rows[PR["w_sc"]:PR["w_sc"] + SC * QF, 0, :], w_sc[0].rearrange("j (f p) -> (j f) p", p=P), "param_in")
            load(rows[0:DW_ROWS, 1, :], w_dw[0].rearrange("j (f p) -> (j f) p", p=P), "param_in")
            load(wab, w_in[0, :, 3072:3080].rearrange("(k p) n -> p k n", p=P), "wab_in")
            load(dtb, dt_bias[0:1, :].to_broadcast([P, H]), "ab_par")
            load(alog, a_log[0:1, :].to_broadcast([P, H]), "ab_par")
            load(short_rows, st_short[0].rearrange("b j c -> (b j) c"), "short_in")
            load(wr, w_router[0].rearrange("(k p) n -> p k n", p=P), "wr_in")
            load(br_bc, b_router[0:1, :].to_broadcast([P, E]), "wr_in")
            chain = [0]

            def link(ins):
                chain[0] += 1
                ins.then_inc(sem("act_step"), 1)
                act.wait_ge(sem("act_step"), chain[0])

            def squares(src, wait, s, width, dst=None):
                for k in range(KT):
                    wait(k)
                    act.activation((mix_sq if dst is None else dst)[:, k, 0:width], src[:, k, 0:width],
                                   ACT.Square).then_inc(sem(s), 1)

            def inv_root(key, out, width, scale, bias=0.0):
                wait_filled(act, *key)
                link(act.activation(lnb[:, 0:width], ps(key)[:, 0:width], ACT.Ln, bias=eps_t[:, 0:1], scale=scale))
                drained(act.activation(out[:, 0:width], lnb[:, 0:width], ACT.Exp, scale=-0.5, bias=bias), key)
                wait_drained(act, *key)

            act.wait_ge(sem("const"), 1)
            squares(xT, lambda k: wait_drained(act, "x_t", k), "x_sq", T)
            inv_root(("mix_norm",), rn[:, 0, :], T, 1.0 / D)

            def softplus_parts():
                act.wait_ge(sem("dt_sum"), 1)
                link(act.activation(ta, tt_, ACT.Abs))
                link(act.activation(ta, ta, ACT.Exp, scale=-1.0))
                link(act.activation(ta, ta, ACT.Ln, bias=eps_t[:, 2:3]))
                link(act.activation(ealog, alog, ACT.Exp))
                act.activation(eb, ab[:, :, 4:8], ACT.Exp, scale=-1.0).then_inc(sem("softplus"), 1)

            def silu_qkv(f):
                act.wait_ge(sem("qkv_conv"), f + 1)
                act.activation(qkv[:, f, :], qkv[:, f, :], ACT.Silu).then_inc(sem("qkv_silu"), 1)

            for f in range(QF):
                wait_filled(act, "qkv", f)
                drained(act.copy(u_raw[:, f, HS:HS + T], ps(("qkv", f))[:, 0:T]), ("qkv", f))
                if f == 0:
                    softplus_parts()
                if f >= 1:
                    silu_qkv(f - 1)
            wait_filled(act, "z", 0)
            drained(act.activation(zg[:, 0, :], ps(("z", 0))[:, 0:T], ACT.Silu), ("z", 0))
            silu_qkv(QF - 1)
            for f in range(2 * H):
                act.wait_ge(sem("qkv_silu"), f + 1)
                act.activation(mix_sq[:, f, :], qkv[:, f, :], ACT.Square).then_inc(sem("qk_sq"), 1)
            act.wait_ge(sem("gs"), 1)
            act.activation(ge, gs, ACT.Exp).then_inc(sem("ge"), 1)
            for c in range(NT):
                wait_filled(act, "decay_row", c)
                act.wait_ge(sem("decay_diff"), c + 1)
                act.activation(q_g[c].rearrange("p h n -> p (h n)"), ps(("decay_row", c))[:, :], ACT.Exp)
                drained(act.activation(decay[c], decay[c], ACT.Exp), ("decay_row", c))
            for c in range(NT):
                wait_filled(act, "beta_row", c)
                drained(act.copy(beta_row[c].rearrange("p h n -> p (h n)"), ps(("beta_row", c))[:, :]),
                        ("beta_row", c))
            for n, f in enumerate((4, 5, 6, 7, 0, 1, 2, 3)):
                if n == 4:
                    wait_filled(act, "z", 1)
                    drained(act.activation(zg[:, 1, :], ps(("z", 1))[:, 0:T], ACT.Silu), ("z", 1))
                if n >= 2:
                    act.wait_ge(sem("unit"), n - 1)
                inv_root(("l2", f), rn[:, n % 2, :], T, 1.0, eps_t[:, 1:2] if f < H else 0.0)
            for i in (2, 3):
                wait_filled(act, "z", i)
                drained(act.activation(zg[:, i, :], ps(("z", i))[:, 0:T], ACT.Silu), ("z", i))

            def glu_gate(i):
                wait_filled(act, "glu_b", i)
                if i >= 2:
                    wait_drained(act, "glu_a", i - 2)
                drained(act.activation(sig[:, i % 2, :], ps(("glu_b", i))[:, 0:T], ACT.Sigmoid,
                                       bias=pcol("b_glu", CF + i)), ("glu_b", i))

            order = sorted(JOB, key=JOB.get)
            for key in order[JOB[("inv_t", 0, 0)]:JOB[("w_neg",)]]:
                if key[0] == "inv_x":
                    lv, c = key[1:]
                    wait_filled(act, *key)
                    drained(act.copy(inv_x[c].rearrange("p h n -> p (h n)"), ps(key)[:, :]), key)
                elif key[0] == "glu_b":
                    glu_gate(key[1])
            wait_filled(act, "w_neg")
            drained(act.mul(w_neg.rearrange("p h n -> p (h n)"), ps(("w_neg",))[:, :], -1.0), ("w_neg",))
            for c in range(NT):
                wait_filled(act, "v_new", c)
                drained(act.copy(v_new[c].rearrange("p h n -> p (h n)"), ps(("v_new", c))[:, :]), ("v_new", c))
            wait_filled(act, "s_decay")
            act.activation(s_eg, ps(("s_decay",))[:, 0:BH], ACT.Exp)
            drained(act.copy(s_beta, ps(("s_decay",))[:, BH:2 * BH]), ("s_decay",))
            wait_drained(act, "s_decay")
            wait_filled(act, "s_read")
            for c in range(BH):
                act.activation(s_state[:, c, :], s_state[:, c, :], ACT.Copy, scale=s_eg[:, c:c + 1]).then_inc(
                    sem("s_state_decayed"), 1)
            for c in range(8):
                wait_filled(act, "mem_t", c)
                drained(act.copy(memT[:, c, :], ps(("mem_t", c))[:, 0:NMEM]), ("mem_t", c))
            squares(memT, lambda k: wait_drained(act, "mem_t", k), "mem_sq", NMEM, mkT)
            inv_root(("mem_norm",), rn[:, 0, :], NMEM, 1.0 / D)
            for j in range(4):
                hf, t = divmod(j, 2)
                wait_filled(act, "mk", j)
                drained(act.copy(mk_tok[:, t, hf * 512:(hf + 1) * 512], ps(("mk", j))[:, :]), ("mk", j))
            wait_drained(act, "s_read")
            for h in range(H):
                wait_drained(act, "o_t", 1)
                act.activation(mix[:, h, :], mix[:, H + h, :], ACT.Square).then_inc(sem("o_sq"), 1)
            for h in range(H):
                if h >= 1:
                    act.wait_ge(sem("o_scaled"), h)
                inv_root(("o_norm", h), rn[:, 1, :], T, 1.0 / P)
            for j in range(4):
                hf, t = divmod(j, 2)
                wait_filled(act, "mv", j)
                drained(act.copy(mv_tok[:, t, hf * 512:(hf + 1) * 512], ps(("mv", j))[:, :]), ("mv", j))
            for j in range(4):
                wait_filled(act, "mk_t", j)
                drained(act.copy(mkT[:, 2 * j:2 * j + 2, :].rearrange("p a b -> p (a b)"), ps(("mk_t", j))[:, :]),
                        ("mk_t", j))
            for j in range(2):
                wait_filled(act, "conv_hist", j)
                drained(act.copy(conv_hist[:, 2 * j:2 * j + 2].rearrange("p f b j -> p (f b j)"),
                                 ps(("conv_hist", j))[:, 0:480]), ("conv_hist", j))
            for j in range(3):
                wait_filled(act, "tail_g", j)
                if j:
                    act.wait_ge(sem("tails_out"), 32 * j)
                drained(act.copy(tail_rows[0:HS + TS, :], ps(("tail_g", j))[0:HS + TS, :]), ("tail_g", j))
            wait_filled(act, "tail_c")
            act.wait_ge(sem("tails_out"), 16 * 6)
            drained(act.copy(tail_rows[0:HC + TS, :], ps(("tail_c",))[0:HC + TS, :]), ("tail_c",))
            wait_drained(act, "ln_mean")
            act.activation(glu[:, :, 0:T], conv, ACT.Square).then_inc(sem("ln_sq"), 1)
            act.wait_ge(sem("o_scaled"), H)
            inv_root(("ln_var",), rn[:, 0, :], T, 1.0 / (CF * P))
            act.wait_ge(sem("ln_scaled"), 1)
            for f in range(CF):
                act.activation(mix[:, f, :], conv[:, f, :], ACT.Silu, scale=pcol("ln_g", f),
                               bias=pcol("ln_b", f)).then_inc(sem("mix_conv"), 1)
            wait_drained(act, "w_out", 7)
            squares(xT, lambda k: None, "x2_sq", T)
            inv_root(("x_norm",), rn[:, 0, :], T, 1.0 / D)
            for d in range(8):
                wait_filled(act, "xq", d)
                drained(act.copy(qT[:, d, :], ps(("xq", d))[:, 0:T]), ("xq", d))
            for j in range(2):
                wait_filled(act, "q_s", j)
                drained(act.copy(q_s[:, j * 512:(j + 1) * 512], ps(("q_s", j))[0:TS, :]), ("q_s", j))
            for t in range(2):
                for hp in range(2):
                    act.wait_ge(sem("neg_max"), 2 * t + hp + 1)
                    for u in range(2):
                        h = 2 * hp + u
                        ins = act.activation(probs[:, t, h, :], ps(("score", t, hp))[:, u * NMEM:(u + 1) * NMEM],
                                             ACT.Exp, scale=XD ** -0.5, bias=nmx[:, 4 * t + h:4 * t + h + 1],
                                             accum_out=ssum[:, 4 * t + h:4 * t + h + 1])
                    drained(ins, ("score", t, hp))
            for t in range(2):
                for hp in range(2):
                    wait_filled(act, "prob_t", t, hp)
                    drained(act.copy(pT[:, 2 * hp:2 * hp + 2, :, t * P:(t + 1) * P],
                                     ps(("prob_t", t, hp))[:, :].rearrange("p (h u t) -> p h u t", h=2, u=2)),
                            ("prob_t", t, hp))
            act.wait_ge(sem("s_neg_max"), 1)
            act.wait_ge(sem("q_scratch"), 16)
            act.activation(s_pr, ps(("s_score_t",))[0:BH, 0:NMEM], ACT.Exp, scale=XD ** -0.5, bias=smx[0:BH, 0:1],
                           accum_out=smx[0:BH, 1:2]).then_inc(sem("s_exp"), 1)
            wait_filled(act, "s_prob_t")
            drained(act.copy(s_pT.rearrange("p m c -> p (m c)"), ps(("s_prob_t",))[:, 0:2 * BH]), ("s_prob_t",))
            wait_drained(act, "xo", 7)
            squares(xT, lambda k: None, "x3_sq", T)
            inv_root(("moe_norm",), rn[:, 0, :], T, 1.0 / D)
            for i in range(6):
                t, hf = divmod(i, 2)
                m = ROWS[t][2]
                wait_filled(act, "h_tok", i)
                drained(act.copy(h_tok[0:m, t, hf * 512:(hf + 1) * 512], ps(("h_tok", i))[0:m, :]), ("h_tok", i))
                if i == 0:
                    act.wait_ge(sem("top8"), 1)
                    for t2 in range(3):
                        act.activation(gate[:, t2, :], lg[:, t2, 0:E], ACT.Exp, bias=neg_top[:, t2:t2 + 1]).then_inc(
                            sem("gate_exp"), 1)
            wait_filled(act, "gate_t")
            drained(act.copy(gateT[0:E, :], ps(("gate_t",))[0:E, 0:T]), ("gate_t",))
            act.wait_ge(sem("routed"), 1)
            n_items = act.value_load(n_items_i[0:1, 0:1], min_val=E, max_val=5 * E)

            def scatter_matrix(i):
                act.wait_ge(sem("scat_t"), i + 1)
                act.copy(scat, bank[6][:, 0:T]).then_inc(sem("scat_sb"), 1)

            def gathered_rows(i):
                act.wait_ge(sem("gathered"), i + 1)
                act.copy(hg_rows, bank[2][:, :]).then_inc(sem("hg_rows_ready"), 1)

            def gathered_columns(i):
                act.wait_ge(sem("hg_t"), i + 1)
                act.copy(hg.rearrange("p c m -> p (c m)"), bank[3][:, :]).then_inc(sem("hg_ready"), 1)

            act.preload_act_table(ACT.Sigmoid)
            gathered_rows(0)
            gathered_columns(0)
            with act.Fori(0, n_items) as i:
                scatter_matrix(i)
                act.wait_ge(sem("glu_clipped"), i + 1)
                act.activation(sg, xg, ACT.Sigmoid, scale=1.702).then_inc(sem("sigmoid"), 1)
                gathered_rows(i + 1)
                act.wait_ge(sem("act_turned"), i + 1)
                act.copy(act_t.rearrange("p c m -> p (c m)"), bank[4][:, :]).then_inc(sem("act_t_ready"), 1)
                gathered_columns(i + 1)
                act.wait_ge(sem("piece_used"), 12 * i + 12)
                act.copy(y_rows, bank[5][:, :]).then_inc(sem("y_ready"), 1)
            scatter_matrix(n_items)

            act.wait_ge(sem("scat_added"), 8 * n_items + 9)
            squares(xT, lambda k: None, "x4_sq", T)
            inv_root(("fin_norm",), rn[:, 0, :], T, 1.0 / D)
            for i in range(6):
                t, hf = divmod(i, 2)
                m = ROWS[t][2]
                wait_filled(act, "y_t", i)
                drained(act.copy(y_out[0:m, t, hf * 512:(hf + 1) * 512], ps(("y_t", i))[0:m, :]), ("y_t", i))

        @block.vector
        def _(dve):
            chain = [0]

            def link(ins):
                chain[0] += 1
                ins.then_inc(sem("dve_step"), 1)
                dve.wait_ge(sem("dve_step"), chain[0])

            def scale_rows(key, dst, src, gain, s, width):
                wait_drained(dve, *key)
                for k in range(KT):
                    dve.scalar_tensor_tensor(out=dst[:, k, 0:width], in0=src[:, k, 0:width], scalar=pcol(gain, k),
                                             in1=rn[:, 0, 0:width], op0=ALU.mult, op1=ALU.mult).then_inc(sem(s), 1)

            dve.memset(u_raw[:, :, 0:HS], 0.0)
            dve.memset(glu[:, :, 0:HC], 0.0)
            link(dve.memset(ab, 0.0))
            for i in range(2):
                n = PAR_ROWS if i == 0 else DW_ROWS
                wait_filled(dve, "param", i)
                drained(dve.tensor_copy(par[:, i, 0:n], ps(("param", i))[:, 0:n]), ("param", i))
            for c in range(8):
                wait_filled(dve, "x_t", c)
                drained(dve.tensor_copy(xT[:, c, :], ps(("x_t", c))[:, 0:T]), ("x_t", c))
            wait_drained(dve, "param", 1)
            wait_drained(dve, "x_t", 7)
            scale_rows(("mix_norm",), hT, xT, "mix", "h_mix", T)
            wait_filled(dve, "short_hist")
            drained(dve.tensor_copy(short_hist.rearrange("p f b j -> p (f b j)"),
                                    ps(("short_hist",))[:, 0:QF * TS * HS]), ("short_hist",))
            wait_filled(dve, "ab")
            dve.wait_ge(sem("ab_par"), 32)
            dve.tensor_copy(ab[:, 0:2, :], ps(("ab",))[:, 0:16].rearrange("p (t n) -> p t n", t=2))
            drained(dve.tensor_copy(ab[0:TS, 2, :], ps(("ab",))[0:TS, 16:24]), ("ab",))
            wait_drained(dve, "ab")
            dve.tensor_tensor(tt_, ab[:, :, 0:4], dtb.unsqueeze(1).to_broadcast([P, 3, H]), ALU.add).then_inc(
                sem("dt_sum"), 1)

            def conv_short(f):
                wait_drained(dve, "qkv", f)
                for j in range(SC):
                    w = pcol("w_sc", j * QF + f)
                    src = u_raw[:, f, j:j + TP]
                    if j == 0:
                        link(dve.tensor_scalar(qkv[:, f, 0:TP], src, w, None, ALU.mult))
                        link(dve.tensor_scalar(qkv[:, f, TP:T], short_hist[:, f, :, 0], w, None, ALU.mult))
                    elif j < HS:
                        link(dve.scalar_tensor_tensor(out=qkv[:, f, TP:T], in0=short_hist[:, f, :, j], scalar=w,
                                                      in1=qkv[:, f, TP:T], op0=ALU.mult, op1=ALU.add))
                    else:
                        link(dve.scalar_tensor_tensor(out=qkv[:, f, TP:T], in0=u_raw[:, f, HS + TP:HS + T], scalar=w,
                                                      in1=qkv[:, f, TP:T], op0=ALU.mult, op1=ALU.add))
                    if j:
                        ins = dve.scalar_tensor_tensor(out=qkv[:, f, 0:TP], in0=src, scalar=w, in1=qkv[:, f, 0:TP],
                                                       op0=ALU.mult, op1=ALU.add)
                        if j < SC - 1:
                            link(ins)
                        else:
                            ins.then_inc(sem("qkv_conv"), 1)

            def gates():
                dve.wait_ge(sem("softplus"), 1)
                link(dve.scalar_tensor_tensor(out=tt_, in0=tt_, scalar=0.0, in1=ta, op0=ALU.max, op1=ALU.add))
                dve.scalar_tensor_tensor(out=g_log, in0=tt_, scalar=-1.0,
                                         in1=ealog.unsqueeze(1).to_broadcast([P, 3, H]), op0=ALU.mult,
                                         op1=ALU.mult).then_inc(sem("g_log"), 1)
                dve.wait_ge(sem("g_log"), 1)
                link(dve.tensor_scalar(eb, eb, 1.0, None, ALU.add))
                link(dve.reciprocal(beta, eb))

            for f in range(QF):
                conv_short(f)
                if f == 1:
                    gates()
            for c in range(NT):
                dve.tensor_tensor(inv_x[c], tri[:, :].unsqueeze(1).to_broadcast([P, H, P]),
                                  g_log[:, c, :].unsqueeze(2).to_broadcast([P, H, P]), ALU.mult).then_inc(
                    sem("decay_row"), 1)
            for c in range(NT):
                dve.tensor_tensor(inv_t[c], ident[:, :].unsqueeze(1).to_broadcast([P, H, P]),
                                  beta[:, c, :].unsqueeze(2).to_broadcast([P, H, P]), ALU.mult).then_inc(
                    sem("beta_row"), 1)
            for j, v in enumerate((g_log, beta)):
                ins = dve.tensor_tensor(s_rhs[0:TS, j * BH:(j + 1) * BH].rearrange("p (b h) -> p b h", b=TS),
                                        ident[0:TS, 0:TS].unsqueeze(2).to_broadcast([TS, TS, H]),
                                        v[0:TS, 2, :].unsqueeze(1).to_broadcast([TS, TS, H]), ALU.mult)
            ins.then_inc(sem("s_rhs"), 1)
            wait_filled(dve, "decay_small")
            drained(dve.tensor_copy(gs[:, 0:16], ps(("decay_small",))[:, 0:16]), ("decay_small",))
            wait_drained(dve, "decay_small")
            dve.tensor_tensor(gs[:, 16:24], gs[:, 8:16], gs[:, 0:8], ALU.subtract).then_inc(sem("gs"), 1)
            for c in range(NT):
                wait_filled(dve, "decay_row", c)
                for h in range(H):
                    ins = dve.tensor_scalar(decay[c][:, h, :], ps(("decay_row", c))[:, h * P:(h + 1) * P],
                                            gs[:, 4 * c + h:4 * c + h + 1], 0.0, ALU.subtract, ALU.min)
                ins.then_inc(sem("decay_diff"), 1)
            dve.wait_ge(sem("ge"), 1)
            link(dve.tensor_tensor(bg.rearrange("p (c h) -> p c h", c=2), beta[:, 0:2, :],
                                   ge[:, 0:8].rearrange("p (c h) -> p c h", c=2), ALU.mult))
            for c in range(NT):
                wait_drained(dve, "decay_row", c)
                link(dve.tensor_tensor(decay[c], decay[c], tri[:, :].unsqueeze(1).to_broadcast([P, H, P]), ALU.mult))
            for n, f in enumerate((4, 5, 6, 7, 0, 1, 2, 3)):
                wait_drained(dve, "l2", f)
                if n >= 1:
                    dve.wait_ge(sem("unit"), n)
                dve.tensor_tensor(qkv[:, f, :], qkv[:, f, :], rn[:, n % 2, :], ALU.mult).then_inc(sem("unit"), 1)
            dve.wait_ge(sem("unit"), 8)
            dve.tensor_tensor(s_kq.rearrange("p (b h) -> p h b", b=TS), qkv[:, 0:H, TP:T], qkv[:, H:2 * H, TP:T],
                              ALU.mult).then_inc(sem("s_kq"), 1)
            dve.wait_ge(sem("unit"), 8)
            dve.tensor_tensor(q_g[1], q_g[1], qkv[:, 0:H, P:2 * P], ALU.mult).then_inc(sem("q_g"), 1)

            def per_head(v, c):
                return v[:, 4 * c:4 * c + 4].unsqueeze(2).to_broadcast([P, H, P])

            def by_head(key):
                return ps(key)[:, :].rearrange("p (h n) -> p h n", h=H)

            for c in range(NT):
                wait_filled(dve, "v_tok", c)
                drained(dve.tensor_tensor(v_beta[c], by_head(("v_tok", c)),
                                          beta[:, c, :].unsqueeze(2).to_broadcast([P, H, P]), ALU.mult), ("v_tok", c))
            for c in range(NT):
                wait_filled(dve, "k_tok", c)
                dve.tensor_tensor(k_bg[c], by_head(("k_tok", c)), per_head(bg, c), ALU.mult)
                drained(dve.tensor_tensor(k_dec[c], by_head(("k_tok", c)), per_head(ge[:, 16:24], c), ALU.mult),
                        ("k_tok", c))
            for c in range(NT):
                wait_filled(dve, "kk", c)
                dve.scalar_tensor_tensor(out=neg_l[c].rearrange("p h n -> p (h n)"), in0=ps(("kk", c))[:, :],
                                         scalar=-1.0, in1=decay[c].rearrange("p h n -> p (h n)"), op0=ALU.mult,
                                         op1=ALU.mult).then_inc(sem(f"drained{job(('kk', c)) % 8}"), 1)
                wait_drained(dve, "kk", c)
                wait_drained(dve, "beta_row", c)
                link(dve.tensor_tensor(neg_l[c], neg_l[c], beta_row[c], ALU.mult))
                link(dve.tensor_copy(inv_u[c], ident[:, :].unsqueeze(1).to_broadcast([P, H, P])))
                dve.wait_ge(sem("masks"), 3 * LEVELS)
                dve.copy_predicated(inv_u[c], masks[:, 0, :].bitcast(U32).unsqueeze(1).to_broadcast([P, H, P]),
                                    neg_l[c]).then_inc(sem("inv_start"), 1)
            for c in range(NT):
                wait_filled(dve, "qk", c)
                dve.tensor_tensor(intra[c], by_head(("qk", c)), decay[c], ALU.mult).then_inc(
                    sem(f"drained{job(('qk', c)) % 8}"), 1)
            order = sorted(JOB, key=JOB.get)
            for key in order[JOB[("inv_t", 0, 0)]:JOB[("w_neg",)]]:
                if key[0] == "inv_t":
                    lv, c = key[1:]
                    wait_filled(dve, *key)
                    drained(dve.tensor_copy(inv_t[c].rearrange("p h n -> p (h n)"), ps(key)[:, :]), key)
                elif key[0] == "inv_d":
                    lv, c = key[1:]
                    wait_filled(dve, *key)
                    drained(dve.copy_predicated(inv_u[c], masks[:, lv, :].bitcast(U32).unsqueeze(1).to_broadcast(
                        [P, H, P]), by_head(key)), key)
                elif key[0] == "glu_a":
                    i = key[1]
                    wait_filled(dve, *key)
                    wait_drained(dve, "glu_b", i)
                    drained(dve.scalar_tensor_tensor(out=glu[:, i, HC:HC + T], in0=ps(key)[:, 0:T],
                                                     scalar=pcol("b_glu", i), in1=sig[:, i % 2, :], op0=ALU.add,
                                                     op1=ALU.mult), key)
            wait_filled(dve, "state", 0)
            drained(dve.tensor_copy(state.rearrange("p h n -> p (h n)"), ps(("state", 0))[:, :]), ("state", 0))
            for c in range(NT):
                wait_filled(dve, "o_t", c)
                drained(dve.tensor_copy(mix[:, H:2 * H, c * P:(c + 1) * P], by_head(("o_t", c))), ("o_t", c))
            wait_filled(dve, "state", 1)
            wait_drained(dve, "state", 0)
            for h in range(H):
                ins = dve.scalar_tensor_tensor(out=state_out[:, h, :], in0=state[:, h, :],
                                               scalar=ge[:, 12 + h:13 + h], in1=ps(("state", 1))[:, h * P:(h + 1) * P],
                                               op0=ALU.mult, op1=ALU.add)
            drained(ins, ("state", 1))
            wait_drained(dve, "s_decay")
            wait_filled(dve, "s_kq")
            drained(dve.tensor_copy(s_kq[:, :], ps(("s_kq",))[:, 0:BH]), ("s_kq",))
            wait_drained(dve, "s_kq")
            wait_filled(dve, "s_read")
            rd = ps(("s_read",))[:, 0:2 * BH].rearrange("p (c j) -> p c j", j=2)
            link(dve.tensor_tensor(s_r, rd[:, :, 1], s_eg, ALU.mult))
            link(dve.tensor_tensor(s_v.rearrange("p (b h) -> p h b", b=TS), qkv[:, 2 * H:3 * H, TP:T],
                                   s_r.rearrange("p (b h) -> p h b", b=TS), ALU.subtract))
            link(dve.tensor_tensor(s_v, s_v, s_beta, ALU.mult))
            dve.tensor_tensor(s_kq, s_kq, s_v, ALU.mult).then_inc(sem("s_vn"), 1)
            link(dve.tensor_tensor(s_o, rd[:, :, 0], s_eg, ALU.mult))
            dve.wait_ge(sem("s_vn"), 1)
            drained(dve.tensor_tensor(mix[:, H:2 * H, TP:T], s_o.rearrange("p (b h) -> p h b", b=TS),
                                      s_kq.rearrange("p (b h) -> p h b", b=TS), ALU.add), ("s_read",))
            for g in range(NG):
                wait_filled(dve, "s_outer", g)
                for j in range(GROUP):
                    c = g * GROUP + j
                    b, h = divmod(c, H)
                    dve.wait_ge(sem("s_state_decayed"), c + 1)
                    ins = dve.scalar_tensor_tensor(out=s_state[:, c, :], in0=ps(("s_outer", g))[:, j * P:(j + 1) * P],
                                                   scalar=qkv[:, H + h, TP + b:TP + b + 1], in1=s_state[:, c, :],
                                                   op0=ALU.mult, op1=ALU.add)
                drained(ins, ("s_outer", g))

            taps = [(f, j) for f in range(CF) for j in range(TAPS)]

            def conv_taps(n):
                for _ in range(n):
                    if not taps:
                        return
                    f, j = taps.pop(0)
                    src = glu[:, f, j:j + TP]
                    if j == 0:
                        wait_drained(dve, "glu_a", f)
                        link(dve.tensor_scalar(conv[:, f, 0:TP], src, dw(0, f), pcol("b_dw", f), ALU.mult, ALU.add))
                    else:
                        link(dve.scalar_tensor_tensor(out=conv[:, f, 0:TP], in0=src, scalar=dw(j, f),
                                                      in1=conv[:, f, 0:TP], op0=ALU.mult, op1=ALU.add))

            scale_rows(("mem_norm",), memT, memT, "mem", "mem_h", NMEM)
            conv_taps(48)
            for h in range(H):
                wait_drained(dve, "o_norm", h)
                dve.scalar_tensor_tensor(out=mix[:, H + h, :], in0=mix[:, H + h, :], scalar=pcol("onorm", 0),
                                         in1=rn[:, 1, :], op0=ALU.mult, op1=ALU.mult).then_inc(sem("o_scaled"), 1)
            dve.wait_ge(sem("o_scaled"), H)
            dve.tensor_tensor(mix[:, H:2 * H, :], mix[:, H:2 * H, :], zg, ALU.mult).then_inc(sem("mix_gdn"), 1)
            conv_taps(len(taps))
            for j in range(2):
                wait_drained(dve, "conv_hist", j)
            for f in range(CF):
                w = par[:, 1, 0:DW_ROWS].rearrange("p (j f) -> p f j", f=CF)[:, f, 0:HC]
                link(dve.tensor_tensor(conv_hist[:, f], conv_hist[:, f], w.unsqueeze(1).to_broadcast([P, TS, HC]),
                                       ALU.mult))
                link(dve.tensor_reduce(conv[:, f, TP:T], conv_hist[:, f], AX.X, ALU.add))
                link(dve.scalar_tensor_tensor(out=conv[:, f, TP:T], in0=glu[:, f, HC + TP:HC + T], scalar=dw(HC, f),
                                              in1=conv[:, f, TP:T], op0=ALU.mult, op1=ALU.add))
                dve.tensor_scalar(conv[:, f, TP:T], conv[:, f, TP:T], pcol("b_dw", f), None, ALU.add).then_inc(
                    sem("conv_done"), 1)
            wait_filled(dve, "ln_mean")
            for f in range(CF):
                ins = dve.scalar_tensor_tensor(out=conv[:, f, :], in0=ps(("ln_mean",))[:, 0:T],
                                               scalar=-1.0 / (CF * P), in1=conv[:, f, :], op0=ALU.mult, op1=ALU.add)
            drained(ins, ("ln_mean",))
            wait_drained(dve, "ln_var")
            dve.tensor_tensor(conv, conv, rn[:, 0, :].unsqueeze(1).to_broadcast([P, CF, T]), ALU.mult).then_inc(
                sem("ln_scaled"), 1)

            def add_to_x(kind, d):
                wait_filled(dve, kind, d)
                drained(dve.tensor_tensor(xT[:, d, :], xT[:, d, :], ps((kind, d))[:, 0:T], ALU.add), (kind, d))

            for d in range(8):
                add_to_x("w_out", d)
            wait_drained(dve, "w_out", 7)
            scale_rows(("x_norm",), hT, xT, "xattn", "h_xattn", T)
            for t in range(2):
                for hp in range(2):
                    wait_filled(dve, "score", t, hp)
                    c = 4 * t + 2 * hp
                    link(dve.tensor_reduce(nmx[:, c:c + 2], ps(("score", t, hp))[:, :].rearrange(
                        "p (h m) -> p h m", h=2), AX.X, ALU.max))
                    dve.tensor_scalar(nmx[:, c:c + 2], nmx[:, c:c + 2], -XD ** -0.5, None, ALU.mult).then_inc(
                        sem("neg_max"), 1)
            for t in range(2):
                for hp in range(2):
                    wait_drained(dve, "score", t, hp)
                    c = 4 * t + 2 * hp
                    link(dve.reciprocal(srec[:, c:c + 2], ssum[:, c:c + 2]))
                    for u in range(2):
                        dve.tensor_scalar(probs[:, t, 2 * hp + u, :], probs[:, t, 2 * hp + u, :],
                                          srec[:, c + u:c + u + 1], None, ALU.mult).then_inc(sem("probs"), 1)
            def s_scores(b):
                dve.wait_ge(sem(f"kv{b % 4}"), 16 * (b // 4 + 1))
                dve.wait_ge(sem(f"q_bc{b % 2}"), 16 * (b // 2 + 1))
                for m in range(2):
                    for h in range(XH):
                        kb = kv[b % 4][:, m, h * XD:(h + 1) * XD]
                        ins = dve.tensor_tensor_reduce(kb, kb, q_bc[:, b % 2, h * XD:(h + 1) * XD], 1.0, 0.0,
                                                       ALU.mult, ALU.add, s_sc[:, m, b * XH + h:b * XH + h + 1])
                ins.then_inc(sem("k_used"), 1)

            for d in range(8):
                wait_filled(dve, "attn", d)
                drained(dve.tensor_copy(oT[:, d, 0:TP], ps(("attn", d))[:, 0:TP]), ("attn", d))
                s_scores(d)
            wait_filled(dve, "s_score_t")
            link(dve.tensor_reduce(smx[0:BH, 0:1], ps(("s_score_t",))[0:BH, 0:NMEM], AX.X, ALU.max))
            dve.tensor_scalar(smx[0:BH, 0:1], smx[0:BH, 0:1], -XD ** -0.5, None, ALU.mult).then_inc(
                sem("s_neg_max"), 1)
            dve.wait_ge(sem("s_exp"), 1)
            drained(dve.reciprocal(smx[0:BH, 2:3], smx[0:BH, 1:2]), ("s_score_t",))
            wait_drained(dve, "s_score_t")
            dve.tensor_scalar(s_pr, s_pr, smx[0:BH, 2:3], None, ALU.mult).then_inc(sem("s_probs"), 1)
            wait_filled(dve, "s_attn")
            drained(dve.tensor_copy(oT[:, :, TP:T], ps(("s_attn",))[:, 0:8 * TS].rearrange("p (d b) -> p d b", d=8)),
                    ("s_attn",))
            for d in range(8):
                add_to_x("xo", d)
            wait_drained(dve, "xo", 7)
            scale_rows(("moe_norm",), hT, xT, "moe", "h_moe", T)
            dve.memset(lg, 0.0)
            link(dve.memset(key8, -1e38))
            link(dve.memset(lg[:, :, E:E + 4], -1e38))
            wait_filled(dve, "logits")
            dve.tensor_tensor(lg[:, 0:2, 0:E], ps(("logits",))[:, 0:2 * E].rearrange("p (t e) -> p t e", t=2),
                              br_bc[:, :].unsqueeze(1).to_broadcast([P, 2, E]), ALU.add)
            drained(dve.tensor_tensor(lg[0:TS, 2, 0:E], ps(("logits",))[0:TS, 2 * E:3 * E], br_bc[0:TS, :], ALU.add),
                    ("logits",))
            wait_drained(dve, "logits")
            for t in range(3):
                link(dve.max(top8[:, t, :], lg[:, t, 0:E]))
            dve.tensor_scalar(neg_top[:, 0:3], top8[:, :, 0], -1.0, None, ALU.mult).then_inc(sem("top8"), 1)
            link(dve.tensor_copy(key8[:, :, 0:4], top8[:, :, 0:4]))
            for t in range(3):
                link(dve.match_replace(lg_rep[:, t, :], key8[:, t, :], lg[:, t, :], 3e38))
            dve.tensor_tensor(mask, lg_rep[:, :, 0:E], lg[:, :, 0:E], ALU.not_equal).then_inc(sem("mask"), 1)
            dve.wait_ge(sem("mask"), 1)
            dve.wait_ge(sem("gate_exp"), 3)
            link(dve.tensor_tensor(gate, gate, mask, ALU.mult))
            link(dve.tensor_reduce(gsum[:, 0:3], gate, AX.X, ALU.add))
            link(dve.reciprocal(gsum[:, 0:3], gsum[:, 0:3]))
            for t in range(3):
                dve.tensor_scalar(gate[:, t, :], gate[:, t, :], gsum[:, t:t + 1], None, ALU.mult).then_inc(
                    sem("gate"), 1)
            wait_filled(dve, "position")
            pp = ps(("position",))
            link(dve.scalar_tensor_tensor(out=posm, in0=pp[:, 0:3 * E].rearrange("p (t e) -> p t e", t=3), scalar=1.0,
                                          in1=mask, op0=ALU.add, op1=ALU.mult))
            link(dve.tensor_scalar(posm, posm, -1.0, None, ALU.add))
            link(dve.tensor_scalar(posm[:, :, E - 1], posm[:, :, E - 1], float(SLOTS), None, ALU.add))
            drained(dve.tensor_reduce(cmax[:, 0:1], pp[:, 3 * E:4 * E], AX.X, ALU.max), ("position",))
            wait_drained(dve, "position")
            link(dve.tensor_scalar(cmax[:, 1:2], cmax[:, 0:1], float(SLOTS), 1.0, ALU.is_gt, ALU.add))
            for b in range(2, 5):
                link(dve.scalar_tensor_tensor(out=cmax[:, b:b + 1],
                                              in0=cmax[:, 0:1], scalar=float(SLOTS * b), in1=cmax[:, b - 1:b],
                                              op0=ALU.is_gt, op1=ALU.add))
            dve.tensor_scalar(n_items_i[:, :], cmax[:, 4:5], float(E), None, ALU.mult).then_inc(sem("routed"), 1)
            for d in range(8):
                add_to_x("b_dn", d)

            for i in range(6):
                wait_drained(dve, "h_tok", i)
            dve.wait_ge(sem("routed"), 1)
            dve.wait_ge(sem("gate"), 3)
            n_items = dve.value_load(n_items_i[0:1, 0:1], min_val=E, max_val=5 * E)
            dve.memset(y_rows, 0.0).then_inc(sem("y_ready"), 1)
            dve.memset(hg_rows, 0.0).then_inc(sem("hg_rows_ready"), 1)
            dve.memset(hg, 0.0).then_inc(sem("hg_ready"), 1)
            dve.memset(xl, 0.0).then_inc(sem("gu_read"), 1)
            dve.memset(act_t, 0.0).then_inc(sem("scat_added"), 1)

            def select(e, i):
                for t in range(3):
                    ins = dve.tensor_scalar(sel[:, t, :], iota[:, 0:SLOTS], posm[:, t, bass.ds(e, 1)], None,
                                            ALU.is_equal)
                ins.then_inc(sem("sel_ready"), 1)

            def select_gates(e, i):
                for t in range(3):
                    ins = dve.tensor_scalar(gsel[:, t, :], iota[:, :], posm[:, t, bass.ds(e, 1)],
                                            gate[:, t, bass.ds(e, 1)], ALU.is_equal, ALU.mult)
                ins.then_inc(sem("gsel_ready"), 1)

            def add_rows(i):
                for n in range(8):
                    u, c = n % 2, n // 2
                    d = 4 * u + c
                    dve.wait_ge(sem("scattered"), 8 * i + (n + 1))
                    dve.tensor_tensor(xT[:, d, :], xT[:, d, :], bank[7 - u][:, 0:T], ALU.add).then_inc(
                        sem("scat_added"), 1)

            def expert_column(e):
                dve.tensor_copy(one_hot, ident[:, bass.ds(e, 1)].to_broadcast([P, SLOTS])).then_inc(sem("one_hot"), 1)

            select(0, 0)
            expert_column(0)
            with dve.Fori(0, n_items) as i:
                prev = (i + (E - 1)) % E
                nxt = (i + 1) % E
                select_gates(prev, i)
                dve.wait_ge(sem("gsel_ready"), i + 1)
                dve.tensor_scalar(posm[:, :, bass.ds(prev, 1)], posm[:, :, bass.ds(prev, 1)], -float(SLOTS), None,
                                  ALU.add).then_inc(sem("pos_moved"), 1)
                dve.wait_ge(sem("pos_moved"), i + 1)
                dve.wait_ge(sem("gathered"), i + 1)
                select(nxt, i + 1)
                dve.wait_ge(sem("piece_used"), 12 * i + 8)
                dve.tensor_scalar(xg, bank[0][:, :], 7.0, None, ALU.min).then_inc(sem("glu_clipped"), 1)
                dve.tensor_scalar(xl, bank[1][:, :], 7.0, -7.0, ALU.min, ALU.max).then_inc(sem("gu_read"), 1)
                dve.wait_ge(sem("gu_read"), i + 2)
                dve.wait_ge(sem("glu_clipped"), i + 1)
                dve.scalar_tensor_tensor(out=xl, in0=xl, scalar=1.0, in1=xg, op0=ALU.add,
                                         op1=ALU.mult).then_inc(sem("glu_step"), 1)
                dve.wait_ge(sem("glu_step"), i + 1)
                dve.wait_ge(sem("sigmoid"), i + 1)
                dve.tensor_tensor(act_rows, xl, sg, ALU.mult).then_inc(sem("act_ready"), 1)
                expert_column(nxt)
                add_rows(i)
            select_gates((n_items + (E - 1)) % E, n_items)
            add_rows(n_items)
            dve.wait_ge(sem("scat_added"), 8 * n_items + 9)
            scale_rows(("fin_norm",), hT, xT, "final", "h_fin", T)


def _log(v):
    import math
    return math.log(v)


_INS = ["x_prompt", "mem_prompt", "x_sample", "state_conformer_conv", "state_gdn_conv", "state_gdn", "cache_mem_k",
        "cache_mem_v", "w_in", "b_glu", "w_dw", "b_dw", "ln_g", "ln_b", "w_sc", "a_log", "dt_bias", "g_onorm",
        "w_out", "g_mix", "g_xattn", "g_mem", "w_xq", "w_mk", "w_mv", "w_xo", "g_moe", "w_router", "b_router",
        "w_gu", "b_gu", "w_dn", "b_dn", "g_final"]
_OUTS = [(1, 256, 1024), (8, 1, 1024), (1, 1, 30, 512), (1, 1, 3, 1536), (1, 1, 4, 128, 128), (1, 1, 256, 4, 256),
         (1, 1, 256, 4, 256), (1, 8, 30, 512), (1, 8, 3, 1536), (1, 8, 4, 128, 128)]


def kernel(**inputs):
    import numpy as _np
    import concourse.bacc as _bacc
    from concourse import mybir as _mybir
    from concourse.bass_utils import run_bass_kernel_spmd as _run

    nc = _bacc.Bacc("TRN2", target_bir_lowering=False, num_devices=1)
    arrays, args = {}, []
    for name in _INS:
        v = _np.ascontiguousarray(inputs[name])
        arrays[f"in_{name}"] = v
        args.append(nc.dram_tensor(f"in_{name}", v.shape, _mybir.dt.from_np(v.dtype), kind="ExternalInput").ap())
    outs = [nc.dram_tensor(f"out_{i}", s, _mybir.dt.float32, kind="ExternalOutput").ap()
            for i, s in enumerate(_OUTS)]
    bass_hymba_step(nc, args, outs)
    r = _run(nc, [arrays], core_ids=[0])
    return tuple(r.results[0][f"out_{i}"] for i in range(len(_OUTS)))
```

```python
import math
from contextlib import ExitStack

import concourse.bass as bass
from concourse import mybir

ALU = mybir.AluOpType
ACT = mybir.ActivationFunctionType
AX = mybir.AxisListType
F32 = mybir.dt.float32
I32 = mybir.dt.int32
U32 = mybir.dt.uint32
P = 128


def pre_moe_jobs(levels, sample_groups):
    jobs = [("x_t", c) for c in range(8)]
    jobs += [("param", 0), ("param", 1), ("mix_norm",), ("short_hist",), ("ab",), ("qkv", 0), ("ab_t",)]
    jobs += [("qkv", f) for f in range(1, 4)] + [("conv_hist", j) for j in range(2)]
    jobs += [("qkv", f) for f in range(4, 12)]
    jobs += [("z", 0), ("decay_small",)]
    jobs += [("decay_row", 0), ("decay_row", 1), ("beta_row", 0), ("beta_row", 1)]
    jobs += [("l2", f) for f in (4, 5, 6, 7, 0, 1, 2, 3)] + [("z", 1), ("kk", 0), ("kk", 1)]
    jobs += [("inv_t", 0, 0), ("inv_t", 0, 1)]
    fill = [[("z", 2)], [("v_tok", 0), ("v_tok", 1)], [("z", 3)], [("k_tok", 0), ("k_tok", 1), ("qk", 0), ("qk", 1)]]
    fill += [[(n, i)] for i in range(4) for n in ("glu_b", "glu_a")]
    for lv in range(1, levels):
        jobs += [("inv_x", lv, 0), ("inv_x", lv, 1)]
        jobs += fill.pop(0)
        jobs += [("inv_d", lv, 0), ("inv_d", lv, 1)]
        if lv < levels - 1:
            jobs += fill.pop(0)
            jobs += [("inv_t", lv, 0), ("inv_t", lv, 1)]
    for f in fill:
        jobs += f
    jobs += [("w_neg",), ("v_new", 0), ("state", 0), ("v_new", 1), ("o_t", 0), ("o_t", 1), ("state", 1)]
    jobs += [("tail_g", j) for j in range(3)] + [("tail_c",)]
    jobs += [("s_decay",), ("s_kq",), ("s_read",)] + [("mem_t", c) for c in range(8)]
    jobs += [("s_outer", g) for g in range(sample_groups)] + [("mem_norm",)]
    jobs += [("mk", t) for t in range(4)]
    jobs += [("o_norm", h) for h in range(4)]
    jobs += [("mv", 0), ("mv", 1)] + [("mk_t", j) for j in range(4)]
    jobs += [("ln_mean",), ("mv", 2), ("ln_var",), ("mv", 3)]
    jobs += [("w_out", d) for d in range(8)] + [("x_norm",)]
    jobs += [("q_s",)] + [("xq", d) for d in range(8)] + [("s_score_t",)]
    for t in range(2):
        jobs += [("score", t, 0), ("score", t, 1)]
    for t in range(2):
        jobs += [("prob_t", t, 0), ("prob_t", t, 1)]
        jobs += [("s_prob_t",)] if t == 0 else [("s_attn", 0)]
    jobs += [("attn", d) for d in range(8)] + [("s_attn", 1), ("s_attn_t",)]
    jobs += [("xo", d) for d in range(8)] + [("moe_norm",)]
    jobs += [("logits",), ("h_tok", 0), ("h_tok", 1), ("logits_t",)] + [("h_tok", i) for i in range(2, 6)]
    jobs += [("position",)]
    return jobs


def bass_hymba_step(nc, a, outs):
    (x_prompt, mem_prompt, x_sample, st_conf, st_short, st_gdn, cache_k, cache_v, w_in, b_glu, w_dw, b_dw,
     ln_g, ln_b, w_sc, a_log, dt_bias, g_onorm, w_out, g_mix, g_xattn, g_mem, w_xq, w_mk, w_mv, w_xo, g_moe,
     w_router, b_router, w_gu, b_gu, w_dn, b_dn, g_final) = a
    (y_prompt, y_sample, o_conf_p, o_short_p, o_gdn_p, o_mem_k, o_mem_v, o_conf_s, o_short_s, o_gdn_s) = outs

    TP = x_prompt.shape[1]
    TS = x_sample.shape[0]
    T = TP + TS
    D = x_prompt.shape[2]
    KT = D // P
    NT = TP // P
    H = st_gdn.shape[2]
    BH = TS * H
    E = w_gu.shape[1]
    TAPS = w_dw.shape[1]
    HC = TAPS - 1
    SC = w_sc.shape[1]
    HS = SC - 1
    QF = w_sc.shape[2] // P
    CF = w_dw.shape[2] // P
    NMEM = mem_prompt.shape[1]
    XH = cache_k.shape[3]
    XD = cache_k.shape[4]
    LEVELS = 7
    SLOTS = 64
    EPS = 1e-6
    SCATTER_BANKS = (7, 6, 0, 1)
    ADD_ORDER = [4 * (n % 2) + n // 2 for n in range(8)]
    GROUP = 4
    NG = BH // GROUP
    ROWS = [(0, 0, P), (1, P, P), (2, TP, TS)]

    with ExitStack() as ctx:
        def sb(name, shape, dt=F32):
            t = ctx.enter_context(nc.sbuf_tensor(name, shape, dt))
            return t[tuple(slice(None) for _ in shape)]

        sems = {}

        def sem(name):
            if name not in sems:
                sems[name] = ctx.enter_context(nc.semaphore(name))
            return sems[name]

        bank = [ctx.enter_context(nc.psum_tensor(f"bank{i}", [P, 512], F32)) for i in range(8)]
        JOB = {key: n for n, key in enumerate(pre_moe_jobs(LEVELS, NG))}
        N_PRE = len(JOB)
        TAIL = {("fin_norm",): 2}
        TAIL.update({("y_t", i): (3 + i) % 8 for i in range(6)})

        def job(key):
            return (N_PRE + (-N_PRE) % 8 + TAIL[key]) if key in TAIL else JOB[key]

        def ps(key):
            return bank[job(key) % 8]

        def open_bank(pe, key):
            n = job(key)
            if key not in TAIL and n >= 8:
                pe.wait_ge(sem(f"drained{n % 8}"), n // 8)

        def uses(key):
            n = job(key)
            if key in TAIL:
                return sum(1 for m in range(N_PRE) if m % 8 == n % 8) + 1
            return n // 8 + 1

        def filled(ins, key):
            ins.then_inc(sem(f"filled{job(key) % 8}"), 1)

        def drained(ins, key):
            ins.then_inc(sem(f"drained{job(key) % 8}"), 1)

        def wait_filled(eng, *key):
            eng.wait_ge(sem(f"filled{job(key) % 8}"), uses(key))

        def wait_drained(eng, *key):
            eng.wait_ge(sem(f"drained{job(key) % 8}"), uses(key))

        ring = sb("ring", [P, 12, 2048])
        region_m = sb("region_m", [P, 8192])
        region_p = sb("region_p", [P, 10560])
        scratch = ring[:, 8:12, :].rearrange("p s n -> p (s n)")

        def carve(base, at, n, dims=None, **sizes):
            v = base[:, at:at + n]
            return v.rearrange(dims, **sizes) if dims else v

        ident = sb("ident", [P, P])
        tri = sb("tri", [P, P])
        tri_strict = sb("tri_strict", [P, P])
        ones = sb("ones", [P, P])
        iota = sb("iota", [P, 2 * SLOTS])
        par = sb("par", [P, 2, P])
        xT = sb("xT", [P, KT, T])
        hT = sb("hT", [P, KT, T])
        mix = sb("mix", [P, KT, T])
        rn = sb("rn", [P, 2, T])
        folded = sb("folded", [P, T])
        fold = sb("fold", [P, E])
        sig = sb("sig", [P, 2, T])
        wab = sb("wab", [P, KT, E])
        wr = sb("wr", [P, KT, E])
        br_bc = sb("br_bc", [P, E])
        small = sb("small", [P, 512])
        eps_t = sb("eps_t", [P, 4])

        inv_len = carve(region_m, 0, 2 * H * T, "p (f t) -> p f t", f=2 * H)
        x_tok = carve(region_m, 0, 3 * D, "p (t d) -> p t d", t=3)
        u_raw = carve(region_p, 0, QF * (HS + T), "p (f t) -> p f t", f=QF)
        qkv = carve(region_p, 3204, QF * T, "p (f t) -> p f t", f=QF)
        rows = carve(region_p, 3204, 2 * P, "p (a n) -> p a n", a=2)
        glu = carve(region_p, 6372, CF * (HC + T), "p (f t) -> p f t", f=CF)
        conv = carve(region_p, 7548, CF * T, "p (f t) -> p f t", f=CF)
        zg = carve(region_p, 8604, H * T, "p (f t) -> p f t", f=H)
        masks = carve(region_p, 9660, LEVELS * P, "p (l n) -> p l n", l=LEVELS)
        short_rows = scratch[0:TS * HS, 0:QF * P]
        short_hist = carve(scratch, 1536, QF * TS * HS, "p (f b j) -> p f b j", f=QF, b=TS)
        mix_sq = mix

        def tiles(base, at):
            return [carve(base, at + c * 512, 512, "p (h n) -> p h n", h=H) for c in range(NT)]

        decay, beta_row, neg_l, inv_x, inv_t = (tiles(scratch, 1024 * i) for i in range(5))
        k_bg, v_beta, k_dec, inv_u, intra, q_g = (tiles(region_m, 1024 * i) for i in range(6))
        v_new = tiles(region_m, 6144)
        w_neg = carve(region_m, 7168, 512, "p (h n) -> p h n", h=H)
        state = carve(region_m, 7680, 512, "p (h n) -> p h n", h=H)
        state_out = carve(scratch, 5120, 512, "p (h n) -> p h n", h=H)
        s_state = carve(scratch, 0, BH * P, "p (c n) -> p c n", c=BH)
        conv_rows = carve(scratch, 5632, 1024, "p (a n) -> p a n", a=2)
        conv_hist = carve(scratch, 6656, CF * TS * HC, "p (f b j) -> p f b j", f=CF, b=TS)
        tail_rows = carve(scratch, 7616, 512)
        tail_g_rows = [conv_rows[0:HS + TS, 0, :], conv_rows[0:HS + TS, 1, :], tail_rows[64:64 + HS + TS, :]]
        memT = carve(region_m, 0, KT * NMEM, "p (c t) -> p c t", c=KT)
        mkT = carve(region_m, 2048, KT * NMEM, "p (c t) -> p c t", c=KT)
        mem_tok = carve(region_m, 4096, 2 * D, "p (t d) -> p t d", t=2)
        mk_tok = mem_tok
        mv_tok = carve(region_m, 6144, 2 * D, "p (t d) -> p t d", t=2)
        qT = carve(region_p, 0, KT * T, "p (c t) -> p c t", c=KT)
        oT = carve(region_p, 2112, KT * T, "p (c t) -> p c t", c=KT)
        probs = carve(region_p, 4224, 2048, "p (t h m) -> p t h m", t=NT, h=XH)
        pT = carve(region_p, 6272, 2048, "p (h u t) -> p h u t", h=XH, u=2)
        q_bc = carve(region_p, 6272, 4096, "p (s n) -> p s n", s=4)
        kv = [v.rearrange("p (t d) -> p t d", t=2)
              for v in [ring[:, 8 + i, :] for i in range(4)] + [region_m[:, 0:2048], region_m[:, 4096:6144]]]
        NKV = len(kv)
        s_sc = sb("s_sc", [P, 2, BH])
        s_pr = mix[0:BH, 0, 0:NMEM]
        q_s = mix[0:TS, 2:6, :].rearrange("p a b -> p (a b)")[:, 0:D]
        s_attn_rows = mix[:, 2:4, :].rearrange("p a b -> p (a b)")[:, 0:512]
        s_pT = mix[:, 6:8, :].rearrange("p a b -> p (a b)")[:, 0:2 * TS * BH].rearrange("p (m b c) -> p m b c", m=2, b=TS)
        x_sq = hT
        h_tok = carve(region_p, 0, 3 * D, "p (t d) -> p t d", t=3)
        y_out = carve(region_p, 0, 3 * D, "p (t d) -> p t d", t=3)
        lg = carve(region_p, 3072, 3 * (E + 4), "p (t e) -> p t e", t=3)
        lg_rep = carve(region_p, 3200, 3 * (E + 4), "p (t e) -> p t e", t=3)
        top8 = carve(region_p, 3328, 24, "p (t e) -> p t e", t=3)
        key8 = carve(region_p, 3360, 24, "p (t e) -> p t e", t=3)
        mask = carve(region_p, 3392, 3 * E, "p (t e) -> p t e", t=3)
        gate = carve(region_p, 3488, 3 * E, "p (t e) -> p t e", t=3)
        posm = carve(region_p, 3584, 3 * E, "p (t e) -> p t e", t=3)
        neg_top = carve(region_p, 3680, 4)
        gsum = carve(region_p, 3688, 4)
        cmax = carve(region_p, 3696, 8)
        sel = carve(region_p, 4000, 3 * SLOTS, "p (t s) -> p t s", t=3)
        gsel = carve(region_p, 4192, 3 * P, "p (t s) -> p t s", t=3)
        scat = carve(region_p, 4576, T)
        one_hot = carve(region_p, 4840, SLOTS)
        hg_rows = carve(region_p, 4904, 512)
        xg = carve(region_p, 5416, 512)
        xl = carve(region_p, 5928, 512)
        sg = carve(region_p, 6440, 512)
        act_rows = carve(region_p, 6952, 512)
        y_rows = carve(region_p, 7464, 512)
        hg = carve(region_p, 7976, 512, "p (c m) -> p c m", c=4)
        act_t = carve(region_p, 8488, 512, "p (c m) -> p c m", c=4)
        b_gu_sb = carve(region_m, 2048, 2 * D)
        b_dn_sb = carve(region_m, 1024, D)
        n_items_i = sb("n_items_i", [P, 1], I32)

        q_scratch = nc.dram_tensor("q_scratch", (TS, D), F32, kind="Internal").ap()

        PR = {}
        at = 0
        for name, n in (("mix", 8), ("xattn", 8), ("mem", 8), ("moe", 8), ("final", 8), ("b_glu", 8),
                        ("b_dw", CF), ("ln_g", CF), ("ln_b", CF), ("onorm", 1), ("w_sc", SC * QF)):
            PR[name] = at
            at += n
        PAR_ROWS = at
        DW_ROWS = TAPS * CF

        def pcol(name, i):
            return par[:, 0, PR[name] + i:PR[name] + i + 1]

        def dw(tap, f):
            return par[:, 1, tap * CF + f:tap * CF + f + 1]

        ab = small[:, 0:24].rearrange("p (t n) -> p t n", t=3)
        dtb = small[:, 24:28]
        alog = small[:, 28:32]
        ealog = small[:, 32:36]
        tt_ = small[:, 36:48].rearrange("p (t n) -> p t n", t=3)
        ta = small[:, 48:60].rearrange("p (t n) -> p t n", t=3)
        g_log = small[:, 60:72].rearrange("p (t n) -> p t n", t=3)
        beta = small[:, 72:84].rearrange("p (t n) -> p t n", t=3)
        eb = small[:, 84:96].rearrange("p (t n) -> p t n", t=3)
        gs = small[:, 96:120]
        ge = small[:, 120:144]
        bg = small[:, 144:152]
        s_rhs = small[:, 160:224]
        s_eg = small[:, 224:256]
        s_beta = small[:, 256:288]
        s_kq = small[:, 288:320]
        s_r = small[:, 320:352]
        s_v = small[:, 352:384]
        s_o = small[:, 384:416]
        nmx = small[:, 416:424]
        ssum = small[:, 424:432]
        srec = small[:, 432:440]
        smx = small[:, 440:444]

        def cols(w, c0):
            return w[0, :, c0:c0 + 512].rearrange("(k p) n -> p k n", p=P)

        GROUPS = [("qkv", w_in, 1024), ("qkv", w_in, 1536), ("qkv", w_in, 2048), ("z", w_in, 2560),
                  ("glu_b", w_in, 512), ("glu_a", w_in, 0), ("mk", w_mk, 0), ("mk", w_mk, 512),
                  ("mv", w_mv, 0), ("mv", w_mv, 512), ("w_out", w_out, 0), ("w_out", w_out, 512),
                  ("xq", w_xq, 0), ("xq", w_xq, 512), ("xo", w_xo, 0), ("xo", w_xo, 512)]
        LAST = [("qkv", 3), ("qkv", 7), ("qkv", 11), ("z", 3), ("glu_b", 3), ("glu_a", 3), ("mk", 1), ("mk", 3),
                ("mv", 1), ("mv", 3), ("w_out", 3), ("w_out", 7), ("xq", 3), ("xq", 7), ("xo", 3), ("xo", 7)]

        def wslot(g):
            return ring[:, 2 * (g % 4):2 * (g % 4) + 2, :].rearrange("p s n -> p (s n)").rearrange(
                "p (k n) -> p k n", k=KT)

        block = ctx.enter_context(nc.Block())

        def gu_piece(e, k):
            return w_gu[0, e, k * P:(k + 1) * P, :]

        def dn_piece(e, j):
            return w_dn[0, e, 2 * j * P:2 * (j + 1) * P, :].rearrange("(t p) n -> p t n", p=P)

        @block.sync
        def _(sp):
            sp.dma_start(x_tok[:, 0:2, :], x_prompt[0].rearrange("(t p) d -> p t d", p=P)).then_inc(sem("x_in"), 16)
            sp.dma_start(x_tok[0:TS, 2, :], x_sample[:, 0, :]).then_inc(sem("x_in"), 16)
            def load_kv(i):
                if i == 0:
                    sp.wait_ge(sem("s_state_out"), 16)
                    sp.wait_ge(sem("tails_out"), 16 * 8)
                    sp.wait_ge(sem("conv_done"), CF)
                    sp.wait_ge(sem("state_p_out"), 16)
                if i == 4:
                    wait_filled(sp, "mv", 3)
                if i == 5:
                    wait_filled(sp, "mk_t", 3)
                    sp.wait_ge(sem("mk_out"), 16)
                if i >= NKV:
                    j = i - NKV
                    if j < TS:
                        sp.wait_ge(sem("k_used"), j + 1)
                    else:
                        sp.wait_ge(sem("v_used"), j - TS + 1)
                src = (cache_k if i < TS else cache_v)[0, i % TS].rearrange("(t p) h d -> p t (h d)", p=P)
                sp.dma_start(kv[i % NKV], src).then_inc(sem(f"kv{i % NKV}"), 16)

            for g, (_, w, c0) in enumerate(GROUPS):
                if g == 14:
                    for i in range(NKV):
                        load_kv(i)
                if g == 1:
                    sp.wait_ge(sem("param_in"), 16 * 12)
                    sp.wait_ge(sem("wab_in"), 16)
                if g >= 4:
                    wait_filled(sp, *LAST[g - 4])
                sp.dma_start(wslot(g), cols(w, c0)).then_inc(sem(f"group{g % 4}"), 16)
                if g == 8:
                    wait_drained(sp, "inv_d", LEVELS - 1, 1)
                    sp.dma_start(s_state, st_gdn[0].rearrange("b h k v -> k (b h) v")).then_inc(sem("s_state_in"), 16)
                    wait_drained(sp, "state", 1)
                    wait_drained(sp, "o_t", 1)
                    sp.dma_start(mem_tok, mem_prompt[0].rearrange("(t p) d -> p t d", p=P)).then_inc(sem("mem_in"), 16)
            for i in range(NKV, 2 * TS):
                load_kv(i)
            for s in (0, 1, 2, 3, 8, 9, 10, 11, 4, 5, 6, 7):
                if s < 8:
                    wait_filled(sp, *LAST[12 + s // 2])
                elif s == 8:
                    wait_filled(sp, "s_attn", 1)
                src = gu_piece(0, s) if s < 8 else dn_piece(0, s - 8)
                dst = ring[:, s, :] if s < 8 else ring[:, s, :].rearrange("p (t n) -> p t n", t=2)
                sp.dma_start(dst, src).then_inc(sem(f"piece{s}"), 16)
            sp.wait_ge(sem("routed"), 1)
            n = sp.value_load(n_items_i[0:1, 0:1], min_val=E, max_val=5 * E)
            with sp.Fori(1, n) as i:
                e = i % E
                for s in range(12):
                    sp.wait_ge(sem("piece_used"), 12 * i + (s - 11))
                    src = gu_piece(e, s) if s < 8 else dn_piece(e, s - 8)
                    dst = ring[:, s, :] if s < 8 else ring[:, s, :].rearrange("p (t n) -> p t n", t=2)
                    sp.dma_start(dst, src).then_inc(sem(f"piece{s}"), 16)

        @block.gpsimd
        def _(pool):
            pool.memset(ident[:, :], 0.0)
            pool.memset(ones[:, :], 1.0)
            pool.memset(tri[:, :], 1.0)
            pool.memset(tri_strict[:, :], 1.0)
            pool.memset(masks, 0.0)
            pool.memset(eps_t[:, 0:1], EPS)
            pool.memset(eps_t[:, 1:2], -0.5 * math.log(P))
            pool.memset(eps_t[:, 2:3], 1.0)
            pool.memset(wab[:, :, 2 * H:E], 0.0)
            pool.iota(iota[:, :], [[0, 2], [1, SLOTS]], 0, 0, allow_small_or_imprecise_dtypes=True).then_inc(sem("const0"), 1)
            pool.wait_ge(sem("const0"), 1)
            pool.affine_select(out=ident[:, :], in_=ident[:, :], compare_op=ALU.not_equal, fill=1.0, base=0,
                               pattern=[[-1, P]], channel_multiplier=1)
            pool.affine_select(out=tri[:, :], in_=tri[:, :], compare_op=ALU.is_ge, fill=0.0, base=0,
                               pattern=[[1, P]], channel_multiplier=-1)
            pool.affine_select(out=tri_strict[:, :], in_=tri_strict[:, :], compare_op=ALU.is_gt, fill=0.0, base=0,
                               pattern=[[1, P]], channel_multiplier=-1).then_inc(sem("const"), 1)
            for lv in range(LEVELS):
                s = 1 << lv
                v = masks[:, lv, :].rearrange("p (b u r) -> p b u r", u=2, r=s)[:, :, 1, :]
                pool.memset(v, 1.0).then_inc(sem("masks"), 1)
                pool.wait_ge(sem("masks"), 3 * lv + 1)
                pool.affine_select(out=v, in_=v, compare_op=ALU.is_ge, fill=0.0, base=0,
                                   pattern=[[-2 * s, P // (2 * s)], [0, s]], channel_multiplier=1).then_inc(
                    sem("masks"), 1)
                pool.wait_ge(sem("masks"), 3 * lv + 2)
                pool.affine_select(out=v, in_=v, compare_op=ALU.is_ge, fill=0.0, base=s - 1,
                                   pattern=[[2 * s, P // (2 * s)], [0, s]], channel_multiplier=-1).then_inc(
                    sem("masks"), 1)
            pool.dma_start(o_conf_s[0, :, 0:HC - 1, :], st_conf[0, :, 1:HC, :]).then_inc(sem("stores"), 16)
            pool.dma_start(o_short_s[0, :, 0:HS - 1, :], st_short[0, :, 1:HS, :]).then_inc(sem("stores"), 16)
            wait_drained(pool, "state", 1)
            pool.dma_start(o_gdn_p[0, 0].rearrange("h k v -> k h v"), state_out).then_inc(sem("state_p_out"), 16)
            for j in range(3):
                wait_drained(pool, "tail_g", j)
                c0 = j * 512
                pool.dma_start(o_short_p[0, 0, :, c0:c0 + 512], tail_g_rows[j][0:HS, :]).then_inc(sem("tails_out"), 16)
                pool.dma_start(o_short_s[0, :, HS - 1, c0:c0 + 512], tail_g_rows[j][HS:HS + TS, :]).then_inc(
                    sem("tails_out"), 16)
            wait_drained(pool, "tail_c")
            pool.dma_start(o_conf_p[0, 0], tail_rows[0:HC, :]).then_inc(sem("tails_out"), 16)
            pool.dma_start(o_conf_s[0, :, HC - 1, :], tail_rows[HC:HC + TS, :]).then_inc(sem("tails_out"), 16)
            wait_drained(pool, "s_decay")
            pool.wait_ge(sem("s_state_in"), 16)
            wait_filled(pool, "s_read")
            for g in range(2):
                v = s_state[:, g * BH // 2:(g + 1) * BH // 2, :]
                pool.tensor_tensor(v, v, s_eg[:, g * BH // 2:(g + 1) * BH // 2].unsqueeze(2).to_broadcast(
                    [P, BH // 2, P]), ALU.mult).then_inc(sem("s_state_decayed"), 1)
            for g in range(NG):
                wait_drained(pool, "s_outer", g)
            pool.dma_start(o_gdn_s[0].rearrange("b h k v -> k (b h) v"), s_state).then_inc(sem("s_state_out"), 16)
            for t in range(2):
                for hf in range(2):
                    wait_drained(pool, "mk", 2 * hf + t)
            pool.dma_start(o_mem_k[0, 0].rearrange("(t p) h d -> p t (h d)", p=P), mk_tok).then_inc(sem("mk_out"), 16)
            for t in range(4):
                wait_drained(pool, "mv", t)
            pool.dma_start(o_mem_v[0, 0].rearrange("(t p) h d -> p t (h d)", p=P), mv_tok).then_inc(sem("mv_out"), 16)
            wait_drained(pool, "q_s")
            pool.dma_start(q_scratch, q_s).then_inc(sem("q_scratch"), 16)
            pool.wait_ge(sem("q_scratch"), 16)
            for b in range(TS):
                if b >= 4:
                    pool.wait_ge(sem("k_used"), b - 3)
                pool.dma_start(q_bc[:, b % 4, :], q_scratch[b:b + 1, :].to_broadcast([P, D])).then_inc(
                    sem(f"q_bc{b % 4}"), 16)
            for d in range(8):
                wait_drained(pool, "attn", d)
            wait_filled(pool, "s_attn", 1)
            pool.wait_ge(sem("mk_out"), 16)
            pool.wait_ge(sem("mv_out"), 16)
            pool.memset(b_gu_sb, 0.0)
            pool.memset(b_dn_sb, 0.0).then_inc(sem("biases_zero"), 1)
            pool.wait_ge(sem("biases_zero"), 1)
            pool.dma_start(b_gu_sb[0:E, :], b_gu[0]).then_inc(sem("b_gu_in"), 16)
            pool.dma_start(b_dn_sb[0:E, :], b_dn[0]).then_inc(sem("b_dn_in"), 16)
            pool.wait_ge(sem("stores"), 32)
            for t, r0, m in ROWS:
                wait_drained(pool, "y_t", 2 * t)
                wait_drained(pool, "y_t", 2 * t + 1)
                dst = y_prompt[0, r0:r0 + P, :] if t < 2 else y_sample[:, 0, :]
                pool.dma_start(dst, y_out[0:m, t, :]).then_inc(sem("stores"), 16)
            pool.wait_ge(sem("stores"), 16 * 5)

        @block.tensor
        def _(pe):
            def project(key, g, f, src, width, ready=None):
                open_bank(pe, key)
                pe.wait_ge(sem(f"group{g % 4}"), 16 * (g // 4 + 1))
                w = wslot(g)
                for k in range(KT):
                    if ready is not None:
                        pe.wait_ge(sem(ready), k + 1)
                    m = pe.matmul(ps(key)[:, 0:width], w[:, k, f * P:(f + 1) * P], src[:, k, 0:width],
                                  start=(k == 0), stop=(k == KT - 1))
                filled(m, key)

            def column_sums(key, sq, n, width, ready=None, order=range(KT)):
                open_bank(pe, key)
                for i, k in enumerate(order[:n]):
                    if ready is not None:
                        pe.wait_ge(sem(ready), i + 1)
                    m = pe.matmul(ps(key)[:, 0:width], ones[:, :], sq[:, k, 0:width], start=(i == 0), stop=(i == n - 1))
                filled(m, key)

            def narrow(key, w, ready):
                open_bank(pe, key)
                for k in range(KT):
                    pe.wait_ge(sem(ready), k + 1)
                    j = k % 4
                    m = pe.matmul(ps(key)[j * E:(j + 1) * E, 0:T], w[:, k, :], hT[:, k, :], start=(k < 4),
                                  stop=(k >= 4))
                filled(m, key)

            def fold_rows(key, src, n):
                open_bank(pe, key)
                wait_drained(pe, src)
                pe.wait_ge(sem("fold"), 1)
                for t, r0, m in ROWS:
                    ins = pe.matmul(ps(key)[0:m, n * t:n * t + n], folded[:, r0:r0 + m], fold[:, 0:n], start=True,
                                    stop=True)
                filled(ins, key)

            for key in sorted(JOB, key=JOB.get):
                kind = key[0]
                if kind == "param":
                    if key[1] == 0:
                        pe.wait_ge(sem("param_in"), 16 * 12)
                    n = PAR_ROWS if key[1] == 0 else DW_ROWS
                    open_bank(pe, key)
                    filled(pe.transpose(ps(key)[:, 0:n], rows[0:n, key[1], :], ident[0:n, 0:n]), key)
                elif kind == "x_t":
                    c = key[1]
                    if c == 0:
                        pe.wait_ge(sem("const"), 1)
                        pe.wait_ge(sem("x_in"), 32)
                    open_bank(pe, key)
                    for t, r0, m in ROWS:
                        ins = pe.transpose(ps(key)[:, r0:r0 + m], x_tok[0:m, t, c * P:(c + 1) * P], ident[0:m, 0:m])
                    filled(ins, key)
                elif kind == "mix_norm":
                    column_sums(key, mix_sq, KT, T, "x_sq")
                elif kind == "short_hist":
                    open_bank(pe, key)
                    pe.wait_ge(sem("short_in"), 16)
                    n = TS * HS
                    for f in range(QF):
                        ins = pe.transpose(ps(key)[:, f * n:(f + 1) * n], short_rows[:, f * P:(f + 1) * P],
                                           ident[0:n, 0:n])
                    filled(ins, key)
                elif kind == "ab":
                    pe.wait_ge(sem("wab_in"), 16)
                    narrow(key, wab, "h_mix")
                elif kind == "ab_t":
                    fold_rows(key, "ab", 2 * H)
                elif kind == "qkv":
                    project(key, key[1] // 4, key[1] % 4, hT, T, "h_mix")
                elif kind == "z":
                    project(key, 3, key[1], hT, T)
                elif kind == "glu_b":
                    project(key, 4, key[1], hT, T)
                elif kind == "glu_a":
                    project(key, 5, key[1], hT, T)
                elif kind == "decay_small":
                    open_bank(pe, key)
                    pe.wait_ge(sem("g_log"), 1)
                    for c in range(NT):
                        pe.matmul(ps(key)[:, 4 * c:4 * c + 4], tri[:, :], g_log[:, c, :], start=True, stop=True)
                    for c in range(NT):
                        ins = pe.matmul(ps(key)[:, 8 + 4 * c:12 + 4 * c], ones[:, :], g_log[:, c, :], start=True,
                                        stop=True)
                    filled(ins, key)
                elif kind in ("decay_row", "beta_row"):
                    c = key[1]
                    src = (inv_x if kind == "decay_row" else inv_t)[c]
                    open_bank(pe, key)
                    pe.wait_ge(sem(kind), c + 1)
                    filled(pe.matmul(ps(key)[:, :], ones[:, :], src.rearrange("p h n -> p (h n)"), start=True,
                                     stop=True), key)
                elif kind == "l2":
                    f = key[1]
                    open_bank(pe, key)
                    pe.wait_ge(sem("qk_sq"), f + 1)
                    filled(pe.matmul(ps(key)[:, 0:T], ones[:, :], mix_sq[:, f, :], start=True, stop=True), key)
                elif kind in ("v_tok", "k_tok"):
                    c = key[1]
                    open_bank(pe, key)
                    if kind == "v_tok":
                        pe.wait_ge(sem("qkv_silu"), QF)
                    else:
                        pe.wait_ge(sem("unit"), H)
                    f0 = 2 * H if kind == "v_tok" else H
                    for h in range(H):
                        ins = pe.transpose(ps(key)[:, h * P:(h + 1) * P], qkv[:, f0 + h, c * P:(c + 1) * P],
                                           ident[:, :])
                    filled(ins, key)
                elif kind in ("kk", "qk"):
                    c = key[1]
                    open_bank(pe, key)
                    pe.wait_ge(sem("unit"), H if kind == "kk" else 2 * H)
                    for h in range(H):
                        k_c = qkv[:, H + h, c * P:(c + 1) * P]
                        r = k_c if kind == "kk" else qkv[:, h, c * P:(c + 1) * P]
                        ins = pe.matmul(ps(key)[:, h * P:(h + 1) * P], k_c, r, start=True, stop=True)
                    filled(ins, key)
                elif kind == "inv_t":
                    lv, c = key[1:]
                    open_bank(pe, key)
                    if lv == 0:
                        pe.wait_ge(sem("inv_start"), c + 1)
                    else:
                        wait_drained(pe, "inv_d", lv, c)
                    for h in range(H):
                        ins = pe.transpose(ps(key)[:, h * P:(h + 1) * P], inv_u[c][:, h, :], ident[:, :])
                    filled(ins, key)
                elif kind == "inv_x":
                    lv, c = key[1:]
                    open_bank(pe, key)
                    wait_drained(pe, "inv_t", lv - 1, c)
                    for h in range(H):
                        ins = pe.matmul(ps(key)[:, h * P:(h + 1) * P], neg_l[c][:, h, :], inv_t[c][:, h, :],
                                        start=True, stop=True)
                    filled(ins, key)
                elif kind == "inv_d":
                    lv, c = key[1:]
                    open_bank(pe, key)
                    wait_drained(pe, "inv_x", lv, c)
                    for h in range(H):
                        ins = pe.matmul(ps(key)[:, h * P:(h + 1) * P], inv_x[c][:, h, :], inv_u[c][:, h, :],
                                        start=True, stop=True)
                    filled(ins, key)
                elif kind == "w_neg":
                    open_bank(pe, key)
                    wait_drained(pe, "inv_d", LEVELS - 1, 0)
                    wait_drained(pe, "inv_d", LEVELS - 1, 1)
                    wait_drained(pe, "k_tok", 1)
                    for h in range(H):
                        ins = pe.matmul(ps(key)[:, h * P:(h + 1) * P], k_bg[1][:, h, :], inv_u[1][:, h, :],
                                        start=True, stop=True)
                    filled(ins, key)
                elif kind == "v_new":
                    c = key[1]
                    open_bank(pe, key)
                    wait_drained(pe, "v_tok", c)
                    if c:
                        wait_drained(pe, "w_neg")
                        wait_drained(pe, "state", 0)
                    for h in range(H):
                        o = ps(key)[:, h * P:(h + 1) * P]
                        ins = pe.matmul(o, inv_u[c][:, h, :], v_beta[c][:, h, :], start=True, stop=(c == 0))
                        if c:
                            ins = pe.matmul(o, w_neg[:, h, :], state[:, h, :], start=False, stop=True)
                    filled(ins, key)
                elif kind == "state":
                    c = key[1]
                    open_bank(pe, key)
                    wait_drained(pe, "v_new", c)
                    wait_drained(pe, "k_tok", c)
                    for h in range(H):
                        ins = pe.matmul(ps(key)[:, h * P:(h + 1) * P], k_dec[c][:, h, :], v_new[c][:, h, :],
                                        start=True, stop=True)
                    filled(ins, key)
                elif kind == "o_t":
                    c = key[1]
                    open_bank(pe, key)
                    wait_drained(pe, "v_new", c)
                    wait_drained(pe, "qk", c)
                    for h in range(H):
                        o = ps(key)[:, h * P:(h + 1) * P]
                        ins = pe.matmul(o, v_new[c][:, h, :], intra[c][:, h, :], start=True, stop=(c == 0))
                        if c:
                            pe.wait_ge(sem("q_g"), 1)
                            ins = pe.matmul(o, state[:, h, :], q_g[1][:, h, :], start=False, stop=True)
                    filled(ins, key)
                elif kind == "s_decay":
                    open_bank(pe, key)
                    pe.wait_ge(sem("s_rhs"), 1)
                    filled(pe.matmul(ps(key)[:, 0:2 * BH], ones[0:TS, :], s_rhs[0:TS, :], start=True, stop=True), key)
                elif kind == "s_kq":
                    open_bank(pe, key)
                    pe.wait_ge(sem("s_kq"), 1)
                    filled(pe.matmul(ps(key)[:, 0:BH], ones[:, :], s_kq[:, :], start=True, stop=True), key)
                elif kind == "s_read":
                    open_bank(pe, key)
                    pe.wait_ge(sem("s_state_in"), 16)
                    for b in range(TS):
                        for h in range(H):
                            c = b * H + h
                            ins = pe.matmul(ps(key)[:, 2 * c:2 * c + 2], s_state[:, c, :],
                                            qkv[:, h:h + H + 1:H, TP + b], start=True, stop=True)
                    filled(ins, key)
                elif kind == "s_outer":
                    open_bank(pe, key)
                    if key[1] == 0:
                        pe.wait_ge(sem("s_vn"), 1)
                    for j in range(GROUP):
                        c = key[1] * GROUP + j
                        ins = pe.matmul(ps(key)[:, j * P:(j + 1) * P], s_v[:, c:c + 1].to_broadcast([P, P]),
                                        ident[:, :], start=True, stop=True)
                    filled(ins, key)
                elif kind == "mem_t":
                    open_bank(pe, key)
                    if key[1] == 0:
                        pe.wait_ge(sem("mem_in"), 16)
                    for t in range(2):
                        ins = pe.transpose(ps(key)[:, t * P:(t + 1) * P], mem_tok[:, t, key[1] * P:(key[1] + 1) * P],
                                           ident[:, :])
                    filled(ins, key)
                elif kind == "mem_norm":
                    column_sums(key, mkT, KT, NMEM, "mem_sq")
                elif kind in ("mk", "mv"):
                    g = (6 if kind == "mk" else 8) + key[1] // 2
                    t = key[1] % 2
                    open_bank(pe, key)
                    pe.wait_ge(sem(f"group{g % 4}"), 16 * (g // 4 + 1))
                    for k in range(KT):
                        pe.wait_ge(sem("mem_h"), k + 1)
                        ins = pe.matmul(ps(key)[:, :], memT[:, k, t * P:(t + 1) * P], wslot(g)[:, k, :],
                                        start=(k == 0), stop=(k == KT - 1))
                    filled(ins, key)
                elif kind == "mk_t":
                    open_bank(pe, key)
                    for t in range(4):
                        wait_drained(pe, "mk", t)
                    for u in range(2):
                        for t in range(2):
                            ct = 2 * key[1] + u
                            ins = pe.transpose(ps(key)[:, (2 * u + t) * P:(2 * u + t + 1) * P],
                                               mk_tok[:, t, ct * P:(ct + 1) * P], ident[:, :])
                    filled(ins, key)
                elif kind == "o_norm":
                    h = key[1]
                    open_bank(pe, key)
                    pe.wait_ge(sem("o_sq"), h + 1)
                    filled(pe.matmul(ps(key)[:, 0:T], ones[:, :], mix[:, h, :], start=True, stop=True), key)
                elif kind == "conv_hist":
                    open_bank(pe, key)
                    pe.wait_ge(sem("conv_rows_in"), 16)
                    for u in range(2):
                        f = 2 * key[1] + u
                        for a2 in range(2):
                            c0 = (2 * u + a2) * 120
                            ins = pe.transpose(ps(key)[:, c0:c0 + 120], conv_rows[0:120, a2, f * P:(f + 1) * P],
                                               ident[0:120, 0:120])
                    filled(ins, key)
                elif kind == "tail_g":
                    open_bank(pe, key)
                    for u in range(4):
                        ins = pe.transpose(ps(key)[0:HS + TS, u * P:(u + 1) * P],
                                           u_raw[:, 4 * key[1] + u, TP:TP + HS + TS], ident[:, :])
                    filled(ins, key)
                elif kind == "tail_c":
                    open_bank(pe, key)
                    for i in range(4):
                        wait_drained(pe, "glu_a", i)
                    for f in range(CF):
                        ins = pe.transpose(ps(key)[0:HC + TS, f * P:(f + 1) * P], glu[:, f, TP:TP + HC + TS],
                                           ident[:, :])
                    filled(ins, key)
                elif kind == "ln_mean":
                    pe.wait_ge(sem("conv_done"), CF)
                    column_sums(key, conv, CF, T)
                elif kind == "ln_var":
                    pe.wait_ge(sem("ln_sq"), 1)
                    column_sums(key, glu, CF, T)
                elif kind == "w_out":
                    if key[1] == 0:
                        pe.wait_ge(sem("mix_conv"), CF)
                        pe.wait_ge(sem("mix_gdn"), 1)
                    project(key, 10 + key[1] // 4, key[1] % 4, mix, T)
                elif kind == "x_norm":
                    column_sums(key, x_sq, KT, T, "x2_sq")
                elif kind == "xq":
                    project(key, 12 + key[1] // 4, key[1] % 4, hT, T)
                elif kind == "q_s":
                    open_bank(pe, key)
                    pe.wait_ge(sem("group0"), 16 * 4)
                    pe.wait_ge(sem("group1"), 16 * 4)
                    for k in range(KT):
                        pe.wait_ge(sem("h_xattn"), k + 1)
                        for h in range(XH):
                            c0 = (h % 2) * XD
                            ins = pe.matmul(ps(key)[32 * h:32 * h + TS, 0:XD], hT[:, k, TP:T],
                                            wslot(12 + h // 2)[:, k, c0:c0 + XD], start=(k == 0), stop=(k == KT - 1))
                    filled(ins, key)
                elif kind == "score":
                    t, hp = key[1:]
                    open_bank(pe, key)
                    for j in range(4):
                        wait_drained(pe, "mk_t", j)
                        wait_drained(pe, "xq", 4 * hp + j)
                    for u in range(2):
                        h = 2 * hp + u
                        for dd in range(2):
                            ins = pe.matmul(ps(key)[:, u * NMEM:(u + 1) * NMEM], qT[:, 2 * h + dd, t * P:(t + 1) * P],
                                            mkT[:, 2 * h + dd, :], start=(dd == 0), stop=(dd == 1))
                    filled(ins, key)
                elif kind == "prob_t":
                    t, hp = key[1:]
                    open_bank(pe, key)
                    pe.wait_ge(sem("probs"), 4 * t + 2 * hp + 2)
                    for u in range(2):
                        for m in range(2):
                            ins = pe.transpose(ps(key)[:, (2 * u + m) * P:(2 * u + m + 1) * P],
                                               probs[:, t, 2 * hp + u, m * P:(m + 1) * P], ident[:, :])
                    filled(ins, key)
                elif kind == "attn":
                    d = key[1]
                    h = d // 2
                    open_bank(pe, key)
                    for t in range(2):
                        wait_drained(pe, "prob_t", t, h // 2)
                    for j in range(4):
                        wait_drained(pe, "mv", j)
                    for m in range(2):
                        ins = pe.matmul(ps(key)[:, 0:TP], mv_tok[:, m, d * P:(d + 1) * P], pT[:, h, m, :],
                                        start=(m == 0), stop=(m == 1))
                    filled(ins, key)
                elif kind == "s_score_t":
                    open_bank(pe, key)
                    pe.wait_ge(sem("k_used"), TS)
                    for m in range(2):
                        ins = pe.transpose(ps(key)[0:BH, m * P:(m + 1) * P], s_sc[:, m, :], ident[:, :])
                    filled(ins, key)
                elif kind == "s_prob_t":
                    open_bank(pe, key)
                    pe.wait_ge(sem("s_probs"), 1)
                    for m in range(2):
                        ins = pe.transpose(ps(key)[:, m * BH:(m + 1) * BH], s_pr[:, m * P:(m + 1) * P],
                                           ident[0:BH, 0:BH])
                    filled(ins, key)
                elif kind == "s_attn":
                    open_bank(pe, key)
                    wait_drained(pe, "s_prob_t")
                    for b in range(4 * key[1], 4 * key[1] + 4):
                        i = TS + b
                        pe.wait_ge(sem(f"kv{i % NKV}"), 16 * (i // NKV + 1))
                        for m in range(2):
                            for n in range(2):
                                j = 2 * m + n
                                ins = pe.matmul(ps(key)[j * BH:(j + 1) * BH, :], s_pT[:, m, b, :],
                                                kv[i % NKV][:, m, n * 512:(n + 1) * 512], start=(b % 4 == 0),
                                                stop=(b % 4 == 3))
                        if b % 4 < 3:
                            ins.then_inc(sem("v_used"), 1)
                    filled(ins, key)
                elif kind == "s_attn_t":
                    open_bank(pe, key)
                    wait_drained(pe, "s_attn", 1)
                    for n in range(4):
                        ins = pe.transpose(ps(key)[:, n * P:(n + 1) * P], s_attn_rows[:, n * P:(n + 1) * P],
                                           ident[:, :])
                    filled(ins, key)
                elif kind == "xo":
                    if key[1] == 0:
                        for d in range(8):
                            wait_drained(pe, "attn", d)
                        wait_drained(pe, "s_attn_t")
                    project(key, 14 + key[1] // 4, key[1] % 4, oT, T)
                elif kind == "moe_norm":
                    column_sums(key, x_sq, KT, T, "x3_sq")
                elif kind == "logits":
                    pe.wait_ge(sem("wr_in"), 32)
                    narrow(key, wr, "h_moe")
                elif kind == "logits_t":
                    fold_rows(key, "logits", E)
                elif kind == "h_tok":
                    t, hf = divmod(key[1], 2)
                    _, r0, m = ROWS[t]
                    open_bank(pe, key)
                    for u in range(4):
                        ins = pe.transpose(ps(key)[0:m, u * P:(u + 1) * P], hT[:, 4 * hf + u, r0:r0 + m], ident[:, :])
                    filled(ins, key)
                elif kind == "position":
                    open_bank(pe, key)
                    pe.wait_ge(sem("mask"), 1)
                    o = ps(key)
                    pe.matmul(o[:, 0:E], tri_strict[:, :], mask[:, 0, :], start=True, stop=True)
                    pe.matmul(o[:, E:2 * E], ones[:, :], mask[:, 0, :], start=True, stop=False)
                    pe.matmul(o[:, E:2 * E], tri_strict[:, :], mask[:, 1, :], start=False, stop=True)
                    pe.matmul(o[:, 2 * E:3 * E], ones[:, :], mask[:, 0, :], start=True, stop=False)
                    pe.matmul(o[:, 2 * E:3 * E], ones[:, :], mask[:, 1, :], start=False, stop=False)
                    pe.matmul(o[:, 2 * E:3 * E], tri_strict[0:TS, :], mask[0:TS, 2, :], start=False, stop=True)
                    pe.matmul(o[:, 3 * E:4 * E], ones[:, :], mask[:, 0, :], start=True, stop=False)
                    pe.matmul(o[:, 3 * E:4 * E], ones[:, :], mask[:, 1, :], start=False, stop=False)
                    filled(pe.matmul(o[:, 3 * E:4 * E], ones[0:TS, :], mask[0:TS, 2, :], start=False, stop=True), key)

            for n in range(max(0, N_PRE - 8), N_PRE):
                pe.wait_ge(sem(f"drained{n % 8}"), n // 8 + 1)
            pe.wait_ge(sem("routed"), 1)
            n_items = pe.value_load(n_items_i[0:1, 0:1], min_val=E, max_val=5 * E)

            def halves(n, lhs, rhs0, rhs1, start, stop):
                for u, rhs in ((0, rhs0), (1, rhs1)):
                    ins = pe.matmul(bank[n][u * SLOTS:(u + 1) * SLOTS, :], lhs, rhs, start=start, stop=stop)
                return ins

            def gather(i):
                pe.wait_ge(sem("sel_ready"), i + 1)
                pe.wait_ge(sem("hg_rows_ready"), i + 1)
                for t, r0, m in ROWS:
                    ins = halves(2, sel[0:m, t, :], h_tok[0:m, t, 0:512], h_tok[0:m, t, 512:1024], t == 0, t == 2)
                ins.then_inc(sem("gathered"), 1)

            def turn(n, dst_bank, s):
                for c in range(4):
                    ins = pe.transpose(bank[dst_bank][:, c * P:(c + 1) * P], n[:, c * P:(c + 1) * P], ident[:, :])
                ins.then_inc(sem(s), 1)

            def turn_gathered(i):
                pe.wait_ge(sem("hg_rows_ready"), i + 2)
                pe.wait_ge(sem("hg_ready"), i + 1)
                turn(hg_rows, 3, "hg_t")

            def turn_gates(i):
                pe.wait_ge(sem("gsel_ready"), i + 1)
                pe.wait_ge(sem("scat_added"), 8 * i + 1)
                for t, r0, m in ROWS:
                    ins = pe.transpose(bank[6][:, r0:r0 + m], gsel[0:m, t, :], ident[0:m, 0:m])
                ins.then_inc(sem("scat_t"), 1)

            def scatter(i):
                pe.wait_ge(sem("scat_sb"), i + 1)
                pe.wait_ge(sem("y_ready"), i + 1)
                for n in range(8):
                    u, c = n % 2, n // 2
                    if n >= 4:
                        pe.wait_ge(sem("scat_added"), 8 * i + (n - 2))
                    pe.matmul(bank[SCATTER_BANKS[n % 4]][:, 0:T], y_rows[u * SLOTS:(u + 1) * SLOTS, c * P:(c + 1) * P],
                              scat[u * SLOTS:(u + 1) * SLOTS, :], start=True, stop=True).then_inc(
                        sem("scattered"), 1)

            gather(0)
            turn_gathered(0)
            pe.wait_ge(sem("b_gu_in"), 16)
            pe.wait_ge(sem("b_dn_in"), 16)
            with pe.Fori(0, n_items) as i:
                pe.wait_ge(sem("one_hot"), i + 1)
                pe.wait_ge(sem("gu_read"), i + 1)
                pe.wait_ge(sem("scat_added"), 8 * i + 1)
                for n in range(2):
                    halves(n, one_hot, b_gu_sb[:, n * D:n * D + 512], b_gu_sb[:, n * D + 512:n * D + 1024], True, False)
                pe.wait_ge(sem("hg_ready"), i + 2)
                for k in range(8):
                    if k == 4:
                        pe.wait_ge(sem("y_ready"), i + 1)
                        halves(5, one_hot, b_dn_sb[:, 0:512], b_dn_sb[:, 512:1024], True, False)
                    pe.wait_ge(sem(f"piece{k}"), 16 * i + 16)
                    x_k = hg[:, k % 4, (k // 4) * SLOTS:(k // 4 + 1) * SLOTS]
                    for n in range(2):
                        ins = halves(n, x_k, ring[:, k, n * D:n * D + 512], ring[:, k, n * D + 512:n * D + 1024],
                                     False, k == 7)
                    ins.then_inc(sem("piece_used"), 1)
                turn_gates(i)
                gather(i + 1)
                pe.wait_ge(sem("act_ready"), i + 1)
                turn(act_rows, 4, "act_turned")
                scatter(i)
                turn_gathered(i + 1)
                pe.wait_ge(sem("act_t_ready"), i + 1)
                for j in range(4):
                    pe.wait_ge(sem(f"piece{8 + j}"), 16 * i + 16)
                    for v in range(2):
                        f = 2 * j + v
                        w = ring[:, 8 + j, v * D:(v + 1) * D]
                        ins = halves(5, act_t[:, f % 4, (f // 4) * SLOTS:(f // 4 + 1) * SLOTS], w[:, 0:512],
                                     w[:, 512:1024], False, f == 7)
                    ins.then_inc(sem("piece_used"), 1)
            turn_gates(n_items)
            scatter(n_items)

            open_bank(pe, ("fin_norm",))
            pe.wait_ge(sem("hg_ready"), n_items + 2)
            column_sums(("fin_norm",), x_sq, KT, T, "x4_sq", ADD_ORDER)
            for i in range(6):
                key = ("y_t", i)
                t, hf = divmod(i, 2)
                _, r0, m = ROWS[t]
                open_bank(pe, key)
                for u in range(4):
                    pe.wait_ge(sem("h_fin"), 4 * hf + u + 1)
                    ins = pe.transpose(ps(key)[0:m, u * P:(u + 1) * P], hT[:, 4 * hf + u, r0:r0 + m], ident[:, :])
                filled(ins, key)

        @block.scalar
        def _(act):
            def load(dst, src, s):
                act.dma_start(dst, src).then_inc(sem(s), 16)

            for name, w, n in (("mix", g_mix, 8), ("xattn", g_xattn, 8), ("mem", g_mem, 8), ("moe", g_moe, 8),
                               ("b_glu", b_glu, 8), ("b_dw", b_dw, CF), ("ln_g", ln_g, CF), ("ln_b", ln_b, CF),
                               ("onorm", g_onorm, 1)):
                load(rows[PR[name]:PR[name] + n, 0, :], w[0].rearrange("(c p) -> c p", p=P), "param_in")
            load(rows[PR["final"]:PR["final"] + 8, 0, :], g_final.rearrange("(c p) -> c p", p=P), "param_in")
            load(rows[PR["w_sc"]:PR["w_sc"] + SC * QF, 0, :], w_sc[0].rearrange("j (f p) -> (j f) p", p=P), "param_in")
            load(rows[0:DW_ROWS, 1, :], w_dw[0].rearrange("j (f p) -> (j f) p", p=P), "param_in")
            load(wab[:, :, 0:2 * H], w_in[0, :, 3072:3080].rearrange("(k p) n -> p k n", p=P), "wab_in")
            load(dtb, dt_bias[0:1, :].to_broadcast([P, H]), "ab_par")
            load(alog, a_log[0:1, :].to_broadcast([P, H]), "ab_par")
            load(short_rows, st_short[0].rearrange("b j c -> (b j) c"), "short_in")
            load(conv_rows[0:120, :, :], st_conf[0].rearrange("b j c -> (b j) c").rearrange("(a p) c -> p a c", a=2),
                 "conv_rows_in")
            load(wr, w_router[0].rearrange("(k p) n -> p k n", p=P), "wr_in")
            load(br_bc, b_router[0:1, :].to_broadcast([P, E]), "wr_in")
            chain = [0]

            def link(ins):
                chain[0] += 1
                ins.then_inc(sem("act_step"), 1)
                act.wait_ge(sem("act_step"), chain[0])

            def squares(src, wait, s, width, dst=None, order=range(KT)):
                for k in order:
                    wait(k)
                    act.activation((mix_sq if dst is None else dst)[:, k, 0:width], src[:, k, 0:width],
                                   ACT.Square).then_inc(sem(s), 1)

            def inv_root(key, width, scale):
                wait_filled(act, *key)
                link(act.activation(rn[:, 1, 0:width], ps(key)[:, 0:width], ACT.Ln, bias=eps_t[:, 0:1], scale=scale))
                drained(act.activation(rn[:, 0, 0:width], rn[:, 1, 0:width], ACT.Exp, scale=-0.5), key)
                wait_drained(act, *key)

            act.wait_ge(sem("const"), 1)
            act.preload_act_table(ACT.Ln)
            squares(xT, lambda k: wait_drained(act, "x_t", k), "x_sq", T)
            inv_root(("mix_norm",), T, 1.0 / D)

            def softplus_parts():
                act.wait_ge(sem("dt_sum"), 1)
                link(act.activation(ta, tt_, ACT.Abs))
                link(act.activation(ta, ta, ACT.Exp, scale=-1.0))
                link(act.activation(ta, ta, ACT.Ln, bias=eps_t[:, 2:3]))
                link(act.activation(ealog, alog, ACT.Exp))
                act.activation(eb, ab[:, :, 4:8], ACT.Exp, scale=-1.0).then_inc(sem("softplus"), 1)

            def silu_qkv(f):
                act.wait_ge(sem("qkv_conv"), f + 1)
                act.activation(qkv[:, f, :], qkv[:, f, :], ACT.Silu).then_inc(sem("qkv_silu"), 1)

            for f in range(QF):
                wait_filled(act, "qkv", f)
                drained(act.copy(u_raw[:, f, HS:HS + T], ps(("qkv", f))[:, 0:T]), ("qkv", f))
                if f == 1:
                    softplus_parts()
                if f == 4:
                    for j in range(2):
                        wait_filled(act, "conv_hist", j)
                        drained(act.copy(conv_hist[:, 2 * j:2 * j + 2].rearrange("p f b j -> p (f b j)"),
                                         ps(("conv_hist", j))[:, 0:480]), ("conv_hist", j))
                if f >= 1:
                    silu_qkv(f - 1)
            def z_copy(i):
                wait_filled(act, "z", i)
                drained(act.copy(zg[:, i, :], ps(("z", i))[:, 0:T]), ("z", i))

            z_copy(0)
            silu_qkv(QF - 1)
            for f in range(2 * H):
                act.wait_ge(sem("qkv_silu"), f + 1)
                act.activation(mix_sq[:, f, :], qkv[:, f, :], ACT.Square).then_inc(sem("qk_sq"), 1)
            act.wait_ge(sem("gs"), 1)
            act.activation(ge, gs, ACT.Exp).then_inc(sem("ge"), 1)
            for c in range(NT):
                wait_filled(act, "decay_row", c)
                act.wait_ge(sem("decay_diff"), c + 1)
                act.activation(q_g[c].rearrange("p h n -> p (h n)"), ps(("decay_row", c))[:, :], ACT.Exp)
                drained(act.activation(decay[c], decay[c], ACT.Exp), ("decay_row", c))
            for c in range(NT):
                wait_filled(act, "beta_row", c)
                drained(act.copy(beta_row[c].rearrange("p h n -> p (h n)"), ps(("beta_row", c))[:, :]),
                        ("beta_row", c))
            for f in (4, 5, 6, 7, 0, 1, 2, 3):
                wait_filled(act, "l2", f)
                drained(act.activation(inv_len[:, f, :], ps(("l2", f))[:, 0:T], ACT.Ln, bias=eps_t[:, 0:1]), ("l2", f))
            for n in (1, 0):
                for f in range(4 * n, 4 * n + 4):
                    wait_drained(act, "l2", f)
                v = inv_len[:, 4 * n:4 * n + 4, :]
                act.activation(v, v, ACT.Exp, scale=-0.5, bias=0.0 if n else eps_t[:, 1:2]).then_inc(
                    sem("inv_len"), 1)
            z_copy(1)

            def glu_gate(i):
                wait_filled(act, "glu_b", i)
                if i >= 2:
                    wait_drained(act, "glu_a", i - 2)
                drained(act.activation(sig[:, i % 2, :], ps(("glu_b", i))[:, 0:T], ACT.Sigmoid,
                                       bias=pcol("b_glu", CF + i)), ("glu_b", i))

            order = sorted(JOB, key=JOB.get)
            for key in order[JOB[("inv_t", 0, 0)]:JOB[("w_neg",)]]:
                if key[0] == "inv_x":
                    lv, c = key[1:]
                    wait_filled(act, *key)
                    drained(act.copy(inv_x[c].rearrange("p h n -> p (h n)"), ps(key)[:, :]), key)
                elif key[0] == "glu_b":
                    glu_gate(key[1])
                elif key[0] == "z":
                    z_copy(key[1])
            for i in range(H):
                wait_drained(act, "z", i)
            wait_filled(act, "w_neg")
            drained(act.mul(w_neg.rearrange("p h n -> p (h n)"), ps(("w_neg",))[:, :], -1.0), ("w_neg",))
            for c in range(NT):
                wait_filled(act, "v_new", c)
                drained(act.copy(v_new[c].rearrange("p h n -> p (h n)"), ps(("v_new", c))[:, :]), ("v_new", c))
            for j in range(3):
                wait_filled(act, "tail_g", j)
                drained(act.copy(tail_g_rows[j], ps(("tail_g", j))[0:HS + TS, :]), ("tail_g", j))
            wait_filled(act, "tail_c")
            drained(act.copy(tail_rows[0:HC + TS, :], ps(("tail_c",))[0:HC + TS, :]), ("tail_c",))
            wait_filled(act, "s_decay")
            act.activation(s_eg, ps(("s_decay",))[:, 0:BH], ACT.Exp)
            drained(act.copy(s_beta, ps(("s_decay",))[:, BH:2 * BH]), ("s_decay",))
            act.preload_act_table(ACT.Ln)
            for c in range(8):
                wait_filled(act, "mem_t", c)
                drained(act.copy(memT[:, c, :], ps(("mem_t", c))[:, 0:NMEM]), ("mem_t", c))
            squares(memT, lambda k: wait_drained(act, "mem_t", k), "mem_sq", NMEM, mkT)
            inv_root(("mem_norm",), NMEM, 1.0 / D)
            act.preload_act_table(ACT.Ln)
            for j in range(4):
                hf, t = divmod(j, 2)
                wait_filled(act, "mk", j)
                drained(act.copy(mk_tok[:, t, hf * 512:(hf + 1) * 512], ps(("mk", j))[:, :]), ("mk", j))
            wait_drained(act, "s_read")
            for h in range(H):
                wait_drained(act, "o_t", 1)
                act.activation(mix[:, h, :], mix[:, H + h, :], ACT.Square).then_inc(sem("o_sq"), 1)
            for h in range(H):
                wait_filled(act, "o_norm", h)
                drained(act.activation(mix[:, h, :], ps(("o_norm", h))[:, 0:T], ACT.Ln, bias=eps_t[:, 0:1],
                                       scale=1.0 / P), ("o_norm", h))
            for h in range(H):
                wait_drained(act, "o_norm", h)
            act.activation(mix[:, 0:H, :], mix[:, 0:H, :], ACT.Exp, scale=-0.5).then_inc(sem("o_inv_root"), 1)
            def mv_copy(j):
                hf, t = divmod(j, 2)
                wait_filled(act, "mv", j)
                drained(act.copy(mv_tok[:, t, hf * 512:(hf + 1) * 512], ps(("mv", j))[:, :]), ("mv", j))

            mv_copy(0)
            mv_copy(1)
            for j in range(4):
                wait_filled(act, "mk_t", j)
                drained(act.copy(mkT[:, 2 * j:2 * j + 2, :].rearrange("p a b -> p (a b)"), ps(("mk_t", j))[:, :]),
                        ("mk_t", j))
            act.preload_act_table(ACT.Ln)
            wait_drained(act, "ln_mean")
            act.activation(glu[:, :, 0:T], conv, ACT.Square).then_inc(sem("ln_sq"), 1)
            mv_copy(2)
            act.wait_ge(sem("o_scaled"), 1)
            inv_root(("ln_var",), T, 1.0 / (CF * P))
            act.activation(zg, zg, ACT.Silu).then_inc(sem("z_silu"), 1)
            act.wait_ge(sem("ln_scaled"), 1)
            for f in range(CF):
                act.activation(mix[:, f, :], conv[:, f, :], ACT.Silu, scale=pcol("ln_g", f),
                               bias=pcol("ln_b", f)).then_inc(sem("mix_conv"), 1)
            act.preload_act_table(ACT.Ln)
            mv_copy(3)
            squares(xT, lambda k: wait_drained(act, "w_out", k), "x2_sq", T, x_sq)
            inv_root(("x_norm",), T, 1.0 / D)
            wait_filled(act, "q_s")
            for h in range(XH):
                ins = act.copy(q_s[:, h * XD:(h + 1) * XD], ps(("q_s",))[32 * h:32 * h + TS, 0:XD])
            drained(ins, ("q_s",))
            act.preload_act_table(ACT.Exp)
            for d in range(8):
                wait_filled(act, "xq", d)
                drained(act.copy(qT[:, d, :], ps(("xq", d))[:, 0:T]), ("xq", d))
            act.wait_ge(sem("s_neg_max"), 1)
            act.wait_ge(sem("q_scratch"), 16)
            act.activation(s_pr, ps(("s_score_t",))[0:BH, 0:NMEM], ACT.Exp, scale=XD ** -0.5, bias=smx[0:BH, 0:1],
                           accum_out=smx[0:BH, 1:2]).then_inc(sem("s_exp"), 1)
            for t in range(2):
                for hp in range(2):
                    act.wait_ge(sem("neg_max"), 2 * t + hp + 1)
                    for u in range(2):
                        h = 2 * hp + u
                        ins = act.activation(probs[:, t, h, :], ps(("score", t, hp))[:, u * NMEM:(u + 1) * NMEM],
                                             ACT.Exp, scale=XD ** -0.5, bias=nmx[:, 4 * t + h:4 * t + h + 1],
                                             accum_out=ssum[:, 4 * t + h:4 * t + h + 1])
                    drained(ins, ("score", t, hp))
            for t in range(2):
                for hp in range(2):
                    wait_filled(act, "prob_t", t, hp)
                    drained(act.copy(pT[:, 2 * hp:2 * hp + 2, :, t * P:(t + 1) * P],
                                     ps(("prob_t", t, hp))[:, :].rearrange("p (h u t) -> p h u t", h=2, u=2)),
                            ("prob_t", t, hp))
            act.preload_act_table(ACT.Ln)
            wait_filled(act, "s_attn", 0)
            drained(act.copy(s_attn_rows, ps(("s_attn", 0))[:, :]), ("s_attn", 0))
            squares(xT, lambda k: wait_drained(act, "xo", k), "x3_sq", T, x_sq)
            inv_root(("moe_norm",), T, 1.0 / D)
            act.preload_act_table(ACT.Exp)
            wait_filled(act, "logits")
            drained(act.copy(folded, ps(("logits",))[:, 0:T]), ("logits",))
            for i in range(6):
                t, hf = divmod(i, 2)
                m = ROWS[t][2]
                wait_filled(act, "h_tok", i)
                drained(act.copy(h_tok[0:m, t, hf * 512:(hf + 1) * 512], ps(("h_tok", i))[0:m, :]), ("h_tok", i))
                if i == 3:
                    act.wait_ge(sem("top8"), 1)
                    for t2 in range(3):
                        act.activation(gate[:, t2, :], lg[:, t2, 0:E], ACT.Exp, bias=neg_top[:, t2:t2 + 1]).then_inc(
                            sem("gate_exp"), 1)
            act.wait_ge(sem("routed"), 1)
            n_items = act.value_load(n_items_i[0:1, 0:1], min_val=E, max_val=5 * E)

            def scatter_matrix(i):
                act.wait_ge(sem("scat_t"), i + 1)
                act.copy(scat, bank[6][:, 0:T]).then_inc(sem("scat_sb"), 1)

            def gathered_rows(i):
                act.wait_ge(sem("gathered"), i + 1)
                act.copy(hg_rows, bank[2][:, :]).then_inc(sem("hg_rows_ready"), 1)

            def gathered_columns(i):
                act.wait_ge(sem("hg_t"), i + 1)
                act.copy(hg.rearrange("p c m -> p (c m)"), bank[3][:, :]).then_inc(sem("hg_ready"), 1)

            act.preload_act_table(ACT.Sigmoid)
            gathered_rows(0)
            gathered_columns(0)
            with act.Fori(0, n_items) as i:
                scatter_matrix(i)
                act.wait_ge(sem("glu_clipped"), i + 1)
                act.activation(sg, xg, ACT.Sigmoid, scale=1.702).then_inc(sem("sigmoid"), 1)
                gathered_rows(i + 1)
                act.wait_ge(sem("act_turned"), i + 1)
                act.copy(act_t.rearrange("p c m -> p (c m)"), bank[4][:, :]).then_inc(sem("act_t_ready"), 1)
                gathered_columns(i + 1)
                act.wait_ge(sem("piece_used"), 12 * i + 12)
                act.copy(y_rows, bank[5][:, :]).then_inc(sem("y_ready"), 1)
            scatter_matrix(n_items)

            act.preload_act_table(ACT.Ln)
            squares(xT, lambda k: act.wait_ge(sem("scat_added"), 8 * n_items + (2 + ADD_ORDER.index(k))), "x4_sq", T,
                    x_sq, ADD_ORDER)
            inv_root(("fin_norm",), T, 1.0 / D)
            for i in range(6):
                t, hf = divmod(i, 2)
                m = ROWS[t][2]
                wait_filled(act, "y_t", i)
                drained(act.copy(y_out[0:m, t, hf * 512:(hf + 1) * 512], ps(("y_t", i))[0:m, :]), ("y_t", i))

        @block.vector
        def _(dve):
            chain = [0]

            def link(ins):
                chain[0] += 1
                ins.then_inc(sem("dve_step"), 1)
                dve.wait_ge(sem("dve_step"), chain[0])

            def scale_rows(key, dst, src, gain, s, width):
                wait_drained(dve, *key)
                for k in range(KT):
                    dve.scalar_tensor_tensor(out=dst[:, k, 0:width], in0=src[:, k, 0:width], scalar=pcol(gain, k),
                                             in1=rn[:, 0, 0:width], op0=ALU.mult, op1=ALU.mult).then_inc(sem(s), 1)

            dve.memset(u_raw[:, :, 0:HS], 0.0)
            dve.memset(glu[:, :, 0:HC], 0.0)
            link(dve.memset(ab, 0.0))
            for c in range(8):
                wait_filled(dve, "x_t", c)
                drained(dve.tensor_copy(xT[:, c, :], ps(("x_t", c))[:, 0:T]), ("x_t", c))
            for i in range(2):
                n = PAR_ROWS if i == 0 else DW_ROWS
                wait_filled(dve, "param", i)
                drained(dve.tensor_copy(par[:, i, 0:n], ps(("param", i))[:, 0:n]), ("param", i))
            dve.tensor_reduce(fold, ident[:, :].rearrange("p (c n) -> p n c", n=E), AX.X, ALU.add).then_inc(
                sem("fold"), 1)
            wait_drained(dve, "param", 1)
            wait_drained(dve, "x_t", 7)
            scale_rows(("mix_norm",), hT, xT, "mix", "h_mix", T)
            wait_filled(dve, "short_hist")
            drained(dve.tensor_copy(short_hist.rearrange("p f b j -> p (f b j)"),
                                    ps(("short_hist",))[:, 0:QF * TS * HS]), ("short_hist",))
            wait_filled(dve, "ab")
            drained(dve.tensor_copy(folded, ps(("ab",))[:, 0:T]), ("ab",))
            wait_filled(dve, "ab_t")
            dve.wait_ge(sem("ab_par"), 32)
            dve.tensor_copy(ab[:, 0:2, :], ps(("ab_t",))[:, 0:16].rearrange("p (t n) -> p t n", t=2))
            drained(dve.tensor_copy(ab[0:TS, 2, :], ps(("ab_t",))[0:TS, 16:24]), ("ab_t",))
            wait_drained(dve, "ab_t")
            dve.tensor_tensor(tt_, ab[:, :, 0:4], dtb.unsqueeze(1).to_broadcast([P, 3, H]), ALU.add).then_inc(
                sem("dt_sum"), 1)

            def conv_short(f):
                wait_drained(dve, "qkv", f)
                for j in range(SC):
                    w = pcol("w_sc", j * QF + f)
                    src = u_raw[:, f, j:j + TP]
                    if j == 0:
                        link(dve.tensor_scalar(qkv[:, f, 0:TP], src, w, None, ALU.mult))
                        link(dve.tensor_scalar(qkv[:, f, TP:T], short_hist[:, f, :, 0], w, None, ALU.mult))
                    elif j < HS:
                        link(dve.scalar_tensor_tensor(out=qkv[:, f, TP:T], in0=short_hist[:, f, :, j], scalar=w,
                                                      in1=qkv[:, f, TP:T], op0=ALU.mult, op1=ALU.add))
                    else:
                        link(dve.scalar_tensor_tensor(out=qkv[:, f, TP:T], in0=u_raw[:, f, HS + TP:HS + T], scalar=w,
                                                      in1=qkv[:, f, TP:T], op0=ALU.mult, op1=ALU.add))
                    if j:
                        ins = dve.scalar_tensor_tensor(out=qkv[:, f, 0:TP], in0=src, scalar=w, in1=qkv[:, f, 0:TP],
                                                       op0=ALU.mult, op1=ALU.add)
                        if j < SC - 1:
                            link(ins)
                        else:
                            ins.then_inc(sem("qkv_conv"), 1)

            def gates():
                dve.wait_ge(sem("softplus"), 1)
                link(dve.scalar_tensor_tensor(out=tt_, in0=tt_, scalar=0.0, in1=ta, op0=ALU.max, op1=ALU.add))
                dve.scalar_tensor_tensor(out=g_log, in0=tt_, scalar=-1.0,
                                         in1=ealog.unsqueeze(1).to_broadcast([P, 3, H]), op0=ALU.mult,
                                         op1=ALU.mult).then_inc(sem("g_log"), 1)
                dve.wait_ge(sem("g_log"), 1)
                link(dve.tensor_scalar(eb, eb, 1.0, None, ALU.add))
                link(dve.reciprocal(beta, eb))

            for f in range(QF):
                conv_short(f)
                if f == 2:
                    gates()
            for c in range(NT):
                dve.tensor_tensor(inv_x[c], tri[:, :].unsqueeze(1).to_broadcast([P, H, P]),
                                  g_log[:, c, :].unsqueeze(2).to_broadcast([P, H, P]), ALU.mult).then_inc(
                    sem("decay_row"), 1)
            for c in range(NT):
                dve.tensor_tensor(inv_t[c], ident[:, :].unsqueeze(1).to_broadcast([P, H, P]),
                                  beta[:, c, :].unsqueeze(2).to_broadcast([P, H, P]), ALU.mult).then_inc(
                    sem("beta_row"), 1)
            for j, v in enumerate((g_log, beta)):
                ins = dve.tensor_tensor(s_rhs[0:TS, j * BH:(j + 1) * BH].rearrange("p (b h) -> p b h", b=TS),
                                        ident[0:TS, 0:TS].unsqueeze(2).to_broadcast([TS, TS, H]),
                                        v[0:TS, 2, :].unsqueeze(1).to_broadcast([TS, TS, H]), ALU.mult)
            ins.then_inc(sem("s_rhs"), 1)
            wait_filled(dve, "decay_small")
            drained(dve.tensor_copy(gs[:, 0:16], ps(("decay_small",))[:, 0:16]), ("decay_small",))
            wait_drained(dve, "decay_small")
            dve.tensor_tensor(gs[:, 16:24], gs[:, 8:16], gs[:, 0:8], ALU.subtract).then_inc(sem("gs"), 1)
            for c in range(NT):
                wait_filled(dve, "decay_row", c)
                for h in range(H):
                    ins = dve.tensor_scalar(decay[c][:, h, :], ps(("decay_row", c))[:, h * P:(h + 1) * P],
                                            gs[:, 4 * c + h:4 * c + h + 1], 0.0, ALU.subtract, ALU.min)
                ins.then_inc(sem("decay_diff"), 1)
            dve.wait_ge(sem("ge"), 1)
            link(dve.tensor_tensor(bg.rearrange("p (c h) -> p c h", c=2), beta[:, 0:2, :],
                                   ge[:, 0:8].rearrange("p (c h) -> p c h", c=2), ALU.mult))
            for c in range(NT):
                wait_drained(dve, "decay_row", c)
                link(dve.tensor_tensor(decay[c], decay[c], tri[:, :].unsqueeze(1).to_broadcast([P, H, P]), ALU.mult))

            def unit_vectors(n, fs):
                dve.wait_ge(sem("inv_len"), n)
                for f in fs:
                    dve.tensor_tensor(qkv[:, f, :], qkv[:, f, :], inv_len[:, f, :], ALU.mult).then_inc(
                        sem("unit"), 1)

            unit_vectors(1, range(H, 2 * H))

            def per_head(v, c):
                return v[:, 4 * c:4 * c + 4].unsqueeze(2).to_broadcast([P, H, P])

            def by_head(key):
                return ps(key)[:, :].rearrange("p (h n) -> p h n", h=H)

            for c in range(NT):
                wait_filled(dve, "kk", c)
                dve.scalar_tensor_tensor(out=neg_l[c].rearrange("p h n -> p (h n)"), in0=ps(("kk", c))[:, :],
                                         scalar=-1.0, in1=decay[c].rearrange("p h n -> p (h n)"), op0=ALU.mult,
                                         op1=ALU.mult).then_inc(sem(f"drained{job(('kk', c)) % 8}"), 1)
                wait_drained(dve, "kk", c)
                wait_drained(dve, "beta_row", c)
                link(dve.tensor_tensor(neg_l[c], neg_l[c], beta_row[c], ALU.mult))
                link(dve.tensor_copy(inv_u[c], ident[:, :].unsqueeze(1).to_broadcast([P, H, P])))
                dve.wait_ge(sem("masks"), 3 * LEVELS)
                dve.copy_predicated(inv_u[c], masks[:, 0, :].bitcast(U32).unsqueeze(1).to_broadcast([P, H, P]),
                                    neg_l[c]).then_inc(sem("inv_start"), 1)

            conv_steps = [(f, j) for pair in ((0, 1), (2, 3)) for j in range(TAPS + 4) for f in pair]
            conv_mark = [chain[0]] * CF

            def conv_some(n):
                for f, j in conv_steps[:n]:
                    dve.wait_ge(sem("dve_step"), conv_mark[f])
                    src = glu[:, f, j:j + TP]
                    sample = conv[:, f, TP:T]
                    if j == 0:
                        wait_drained(dve, "glu_a", f)
                        ins = dve.tensor_scalar(conv[:, f, 0:TP], src, dw(0, f), pcol("b_dw", f), ALU.mult, ALU.add)
                    elif j < TAPS:
                        ins = dve.scalar_tensor_tensor(out=conv[:, f, 0:TP], in0=src, scalar=dw(j, f),
                                                       in1=conv[:, f, 0:TP], op0=ALU.mult, op1=ALU.add)
                    elif j == TAPS:
                        wait_drained(dve, "conv_hist", f // 2)
                        w = par[:, 1, 0:DW_ROWS].rearrange("p (j f) -> p f j", f=CF)[:, f, 0:HC]
                        ins = dve.tensor_tensor(conv_hist[:, f], conv_hist[:, f],
                                                w.unsqueeze(1).to_broadcast([P, TS, HC]), ALU.mult)
                    elif j == TAPS + 1:
                        ins = dve.tensor_reduce(sample, conv_hist[:, f], AX.X, ALU.add)
                    elif j == TAPS + 2:
                        ins = dve.scalar_tensor_tensor(out=sample, in0=glu[:, f, HC + TP:HC + T], scalar=dw(HC, f),
                                                       in1=sample, op0=ALU.mult, op1=ALU.add)
                    else:
                        dve.tensor_scalar(sample, sample, pcol("b_dw", f), None, ALU.add).then_inc(
                            sem("conv_done"), 1)
                        continue
                    chain[0] += 1
                    ins.then_inc(sem("dve_step"), 1)
                    conv_mark[f] = chain[0]
                del conv_steps[:n]

            order = sorted(JOB, key=JOB.get)
            for key in order[JOB[("inv_t", 0, 0)]:JOB[("w_neg",)]]:
                if key[0] == "inv_t" and key[1] >= 4 or key[0] == "inv_d" and key[1] >= 5:
                    conv_some(4)
                if key == ("inv_x", 1, 0):
                    unit_vectors(2, range(H))
                    dve.wait_ge(sem("unit"), 2 * H)
                elif key == ("inv_x", 2, 0):
                    dve.tensor_tensor(s_kq.rearrange("p (b h) -> p h b", b=TS), qkv[:, 0:H, TP:T],
                                      qkv[:, H:2 * H, TP:T], ALU.mult).then_inc(sem("s_kq"), 1)
                    dve.tensor_tensor(q_g[1], q_g[1], qkv[:, 0:H, P:2 * P], ALU.mult).then_inc(sem("q_g"), 1)
                elif key[0] == "v_tok":
                    c = key[1]
                    wait_filled(dve, *key)
                    drained(dve.tensor_tensor(v_beta[c], by_head(key),
                                              beta[:, c, :].unsqueeze(2).to_broadcast([P, H, P]), ALU.mult), key)
                elif key[0] == "k_tok":
                    c = key[1]
                    wait_filled(dve, *key)
                    dve.tensor_tensor(k_bg[c], by_head(key), per_head(bg, c), ALU.mult)
                    drained(dve.tensor_tensor(k_dec[c], by_head(key), per_head(ge[:, 16:24], c), ALU.mult), key)
                elif key[0] == "qk":
                    wait_filled(dve, *key)
                    drained(dve.tensor_tensor(intra[key[1]], by_head(key), decay[key[1]], ALU.mult), key)
                elif key[0] == "inv_t":
                    lv, c = key[1:]
                    wait_filled(dve, *key)
                    drained(dve.tensor_copy(inv_t[c].rearrange("p h n -> p (h n)"), ps(key)[:, :]), key)
                elif key[0] == "inv_d":
                    lv, c = key[1:]
                    wait_filled(dve, *key)
                    drained(dve.copy_predicated(inv_u[c], masks[:, lv, :].bitcast(U32).unsqueeze(1).to_broadcast(
                        [P, H, P]), by_head(key)), key)
                elif key[0] == "glu_a":
                    i = key[1]
                    wait_filled(dve, *key)
                    wait_drained(dve, "glu_b", i)
                    drained(dve.scalar_tensor_tensor(out=glu[:, i, HC:HC + T], in0=ps(key)[:, 0:T],
                                                     scalar=pcol("b_glu", i), in1=sig[:, i % 2, :], op0=ALU.add,
                                                     op1=ALU.mult), key)
            wait_filled(dve, "state", 0)
            drained(dve.tensor_copy(state.rearrange("p h n -> p (h n)"), ps(("state", 0))[:, :]), ("state", 0))
            for c in range(NT):
                wait_filled(dve, "o_t", c)
                drained(dve.tensor_copy(mix[:, H:2 * H, c * P:(c + 1) * P], by_head(("o_t", c))), ("o_t", c))
            wait_filled(dve, "state", 1)
            wait_drained(dve, "state", 0)
            for h in range(H):
                ins = dve.scalar_tensor_tensor(out=state_out[:, h, :], in0=state[:, h, :],
                                               scalar=ge[:, 12 + h:13 + h], in1=ps(("state", 1))[:, h * P:(h + 1) * P],
                                               op0=ALU.mult, op1=ALU.add)
            drained(ins, ("state", 1))
            wait_drained(dve, "s_decay")
            wait_filled(dve, "s_kq")
            drained(dve.tensor_copy(s_kq[:, :], ps(("s_kq",))[:, 0:BH]), ("s_kq",))
            wait_drained(dve, "s_kq")
            wait_filled(dve, "s_read")
            rd = ps(("s_read",))[:, 0:2 * BH].rearrange("p (c j) -> p c j", j=2)
            link(dve.tensor_tensor(s_r, rd[:, :, 1], s_eg, ALU.mult))
            link(dve.tensor_tensor(s_v.rearrange("p (b h) -> p h b", b=TS), qkv[:, 2 * H:3 * H, TP:T],
                                   s_r.rearrange("p (b h) -> p h b", b=TS), ALU.subtract))
            link(dve.tensor_tensor(s_v, s_v, s_beta, ALU.mult))
            dve.tensor_tensor(s_kq, s_kq, s_v, ALU.mult).then_inc(sem("s_vn"), 1)
            link(dve.tensor_tensor(s_o, rd[:, :, 0], s_eg, ALU.mult))
            dve.wait_ge(sem("s_vn"), 1)
            drained(dve.tensor_tensor(mix[:, H:2 * H, TP:T], s_o.rearrange("p (b h) -> p h b", b=TS),
                                      s_kq.rearrange("p (b h) -> p h b", b=TS), ALU.add), ("s_read",))
            for g in range(NG):
                wait_filled(dve, "s_outer", g)
                for j in range(GROUP):
                    c = g * GROUP + j
                    b, h = divmod(c, H)
                    dve.wait_ge(sem("s_state_decayed"), 2 * c // BH + 1)
                    ins = dve.scalar_tensor_tensor(out=s_state[:, c, :], in0=ps(("s_outer", g))[:, j * P:(j + 1) * P],
                                                   scalar=qkv[:, H + h, TP + b:TP + b + 1], in1=s_state[:, c, :],
                                                   op0=ALU.mult, op1=ALU.add)
                drained(ins, ("s_outer", g))

            scale_rows(("mem_norm",), memT, memT, "mem", "mem_h", NMEM)
            conv_some(len(conv_steps))
            dve.wait_ge(sem("o_inv_root"), 1)
            dve.scalar_tensor_tensor(out=mix[:, H:2 * H, :], in0=mix[:, H:2 * H, :], scalar=pcol("onorm", 0),
                                     in1=mix[:, 0:H, :], op0=ALU.mult, op1=ALU.mult).then_inc(sem("o_scaled"), 1)
            dve.wait_ge(sem("o_scaled"), 1)
            wait_filled(dve, "ln_mean")
            for f in range(CF):
                ins = dve.scalar_tensor_tensor(out=conv[:, f, :], in0=ps(("ln_mean",))[:, 0:T],
                                               scalar=-1.0 / (CF * P), in1=conv[:, f, :], op0=ALU.mult, op1=ALU.add)
            drained(ins, ("ln_mean",))
            wait_drained(dve, "ln_var")
            dve.tensor_tensor(conv, conv, rn[:, 0, :].unsqueeze(1).to_broadcast([P, CF, T]), ALU.mult).then_inc(
                sem("ln_scaled"), 1)

            dve.wait_ge(sem("z_silu"), 1)
            dve.tensor_tensor(mix[:, H:2 * H, :], mix[:, H:2 * H, :], zg, ALU.mult).then_inc(sem("mix_gdn"), 1)

            def add_to_x(kind, d):
                wait_filled(dve, kind, d)
                drained(dve.tensor_tensor(xT[:, d, :], xT[:, d, :], ps((kind, d))[:, 0:T], ALU.add), (kind, d))

            for d in range(8):
                add_to_x("w_out", d)
            wait_drained(dve, "w_out", 7)
            scale_rows(("x_norm",), hT, xT, "xattn", "h_xattn", T)
            dve.memset(s_pT, 0.0).then_inc(sem("s_pT_zero"), 1)
            for b in range(TS):
                dve.wait_ge(sem(f"kv{b % NKV}"), 16 * (b // NKV + 1))
                dve.wait_ge(sem(f"q_bc{b % 4}"), 16 * (b // 4 + 1))
                for m in range(2):
                    for h in range(XH):
                        kb = kv[b % NKV][:, m, h * XD:(h + 1) * XD]
                        ins = dve.tensor_tensor_reduce(kb, kb, q_bc[:, b % 4, h * XD:(h + 1) * XD], 1.0, 0.0,
                                                       ALU.mult, ALU.add, s_sc[:, m, b * XH + h:b * XH + h + 1])
                ins.then_inc(sem("k_used"), 1)
            wait_filled(dve, "s_score_t")
            link(dve.tensor_reduce(smx[0:BH, 0:1], ps(("s_score_t",))[0:BH, 0:NMEM], AX.X, ALU.max))
            dve.tensor_scalar(smx[0:BH, 0:1], smx[0:BH, 0:1], -XD ** -0.5, None, ALU.mult).then_inc(
                sem("s_neg_max"), 1)
            dve.wait_ge(sem("s_exp"), 1)
            drained(dve.reciprocal(smx[0:BH, 2:3], smx[0:BH, 1:2]), ("s_score_t",))
            wait_drained(dve, "s_score_t")
            dve.tensor_scalar(s_pr, s_pr, smx[0:BH, 2:3], None, ALU.mult).then_inc(sem("s_probs"), 1)
            for t in range(2):
                for hp in range(2):
                    wait_filled(dve, "score", t, hp)
                    c = 4 * t + 2 * hp
                    link(dve.tensor_reduce(nmx[:, c:c + 2], ps(("score", t, hp))[:, :].rearrange(
                        "p (h m) -> p h m", h=2), AX.X, ALU.max))
                    dve.tensor_scalar(nmx[:, c:c + 2], nmx[:, c:c + 2], -XD ** -0.5, None, ALU.mult).then_inc(
                        sem("neg_max"), 1)
            for t in range(2):
                for hp in range(2):
                    wait_drained(dve, "score", t, hp)
                    c = 4 * t + 2 * hp
                    link(dve.reciprocal(srec[:, c:c + 2], ssum[:, c:c + 2]))
                    for u in range(2):
                        dve.tensor_scalar(probs[:, t, 2 * hp + u, :], probs[:, t, 2 * hp + u, :],
                                          srec[:, c + u:c + u + 1], None, ALU.mult).then_inc(sem("probs"), 1)
            wait_filled(dve, "s_prob_t")
            dve.wait_ge(sem("s_pT_zero"), 1)
            for m in range(2):
                for b in range(TS):
                    c = m * BH + b * XH
                    ins = dve.tensor_copy(s_pT[:, m, b, b * XH:(b + 1) * XH], ps(("s_prob_t",))[:, c:c + XH])
            drained(ins, ("s_prob_t",))
            for d in range(8):
                wait_filled(dve, "attn", d)
                drained(dve.tensor_copy(oT[:, d, 0:TP], ps(("attn", d))[:, 0:TP]), ("attn", d))
            wait_filled(dve, "s_attn", 1)
            wait_drained(dve, "s_attn", 0)
            drained(dve.tensor_tensor(s_attn_rows, s_attn_rows, ps(("s_attn", 1))[:, :], ALU.add), ("s_attn", 1))
            wait_filled(dve, "s_attn_t")
            for d in range(8):
                c = (d % 4) * P + (d // 4) * BH + d // 2
                part = [ps(("s_attn_t",))[:, c + m * 2 * BH:c + m * 2 * BH + BH - XH + 1:XH] for m in range(2)]
                dve.tensor_copy(oT[:, d, TP:T], part[0]).then_inc(sem("s_o_first"), 1)
                dve.wait_ge(sem("s_o_first"), d + 1)
                ins = dve.tensor_tensor(oT[:, d, TP:T], oT[:, d, TP:T], part[1], ALU.add)
            drained(ins, ("s_attn_t",))
            dve.memset(y_rows, 0.0).then_inc(sem("y_ready"), 1)
            dve.memset(hg_rows, 0.0).then_inc(sem("hg_rows_ready"), 1)
            dve.memset(hg, 0.0).then_inc(sem("hg_ready"), 1)
            dve.memset(xl, 0.0).then_inc(sem("gu_read"), 1)
            dve.memset(act_t, 0.0).then_inc(sem("scat_added"), 1)
            for d in range(8):
                add_to_x("xo", d)
            wait_drained(dve, "xo", 7)
            scale_rows(("moe_norm",), hT, xT, "moe", "h_moe", T)
            dve.memset(lg, 0.0)
            link(dve.memset(key8, -1e38))
            link(dve.memset(lg[:, :, E:E + 4], -1e38))
            wait_filled(dve, "logits_t")
            dve.tensor_tensor(lg[:, 0:2, 0:E], ps(("logits_t",))[:, 0:2 * E].rearrange("p (t e) -> p t e", t=2),
                              br_bc[:, :].unsqueeze(1).to_broadcast([P, 2, E]), ALU.add)
            drained(dve.tensor_tensor(lg[0:TS, 2, 0:E], ps(("logits_t",))[0:TS, 2 * E:3 * E], br_bc[0:TS, :], ALU.add),
                    ("logits_t",))
            wait_drained(dve, "logits_t")
            for t in range(3):
                link(dve.max(top8[:, t, :], lg[:, t, 0:E]))
            dve.tensor_scalar(neg_top[:, 0:3], top8[:, :, 0], -1.0, None, ALU.mult).then_inc(sem("top8"), 1)
            link(dve.tensor_copy(key8[:, :, 0:4], top8[:, :, 0:4]))
            for t in range(3):
                link(dve.match_replace(lg_rep[:, t, :], key8[:, t, :], lg[:, t, :], 3e38))
            dve.tensor_tensor(mask, lg_rep[:, :, 0:E], lg[:, :, 0:E], ALU.not_equal).then_inc(sem("mask"), 1)
            dve.wait_ge(sem("mask"), 1)
            dve.wait_ge(sem("gate_exp"), 3)
            link(dve.tensor_tensor(gate, gate, mask, ALU.mult))
            link(dve.tensor_reduce(gsum[:, 0:3], gate, AX.X, ALU.add))
            link(dve.reciprocal(gsum[:, 0:3], gsum[:, 0:3]))
            for t in range(3):
                dve.tensor_scalar(gate[:, t, :], gate[:, t, :], gsum[:, t:t + 1], None, ALU.mult).then_inc(
                    sem("gate"), 1)
            wait_filled(dve, "position")
            pp = ps(("position",))
            link(dve.scalar_tensor_tensor(out=posm, in0=pp[:, 0:3 * E].rearrange("p (t e) -> p t e", t=3), scalar=1.0,
                                          in1=mask, op0=ALU.add, op1=ALU.mult))
            link(dve.tensor_scalar(posm, posm, -1.0, None, ALU.add))
            link(dve.tensor_scalar(posm[:, :, E - 1], posm[:, :, E - 1], float(SLOTS), None, ALU.add))
            drained(dve.tensor_reduce(cmax[:, 0:1], pp[:, 3 * E:4 * E], AX.X, ALU.max), ("position",))
            wait_drained(dve, "position")
            link(dve.tensor_scalar(cmax[:, 1:2], cmax[:, 0:1], float(SLOTS), 1.0, ALU.is_gt, ALU.add))
            for b in range(2, 5):
                link(dve.scalar_tensor_tensor(out=cmax[:, b:b + 1],
                                              in0=cmax[:, 0:1], scalar=float(SLOTS * b), in1=cmax[:, b - 1:b],
                                              op0=ALU.is_gt, op1=ALU.add))
            dve.tensor_scalar(n_items_i[:, :], cmax[:, 4:5], float(E), None, ALU.mult).then_inc(sem("routed"), 1)

            for i in range(6):
                wait_drained(dve, "h_tok", i)
            dve.wait_ge(sem("routed"), 1)
            dve.wait_ge(sem("gate"), 3)
            n_items = dve.value_load(n_items_i[0:1, 0:1], min_val=E, max_val=5 * E)
            def select(e, i):
                for t in range(3):
                    ins = dve.tensor_scalar(sel[:, t, :], iota[:, 0:SLOTS], posm[:, t, bass.ds(e, 1)], None,
                                            ALU.is_equal)
                ins.then_inc(sem("sel_ready"), 1)

            def select_gates(e, i):
                for t in range(3):
                    ins = dve.tensor_scalar(gsel[:, t, :], iota[:, :], posm[:, t, bass.ds(e, 1)],
                                            gate[:, t, bass.ds(e, 1)], ALU.is_equal, ALU.mult)
                ins.then_inc(sem("gsel_ready"), 1)

            def add_rows(i):
                for n in range(8):
                    d = ADD_ORDER[n]
                    dve.wait_ge(sem("scattered"), 8 * i + (n + 1))
                    dve.tensor_tensor(xT[:, d, :], xT[:, d, :], bank[SCATTER_BANKS[n % 4]][:, 0:T], ALU.add).then_inc(
                        sem("scat_added"), 1)

            def expert_column(e):
                dve.tensor_copy(one_hot, ident[:, bass.ds(e, 1)].to_broadcast([P, SLOTS])).then_inc(sem("one_hot"), 1)

            select(0, 0)
            expert_column(0)
            with dve.Fori(0, n_items) as i:
                prev = (i + (E - 1)) % E
                nxt = (i + 1) % E
                select_gates(prev, i)
                dve.wait_ge(sem("gsel_ready"), i + 1)
                dve.tensor_scalar(posm[:, :, bass.ds(prev, 1)], posm[:, :, bass.ds(prev, 1)], -float(SLOTS), None,
                                  ALU.add).then_inc(sem("pos_moved"), 1)
                dve.wait_ge(sem("pos_moved"), i + 1)
                dve.wait_ge(sem("gathered"), i + 1)
                select(nxt, i + 1)
                dve.wait_ge(sem("piece_used"), 12 * i + 8)
                dve.tensor_scalar(xg, bank[0][:, :], 7.0, None, ALU.min).then_inc(sem("glu_clipped"), 1)
                dve.tensor_scalar(xl, bank[1][:, :], 7.0, -7.0, ALU.min, ALU.max).then_inc(sem("gu_read"), 1)
                dve.wait_ge(sem("gu_read"), i + 2)
                dve.wait_ge(sem("glu_clipped"), i + 1)
                dve.scalar_tensor_tensor(out=xl, in0=xl, scalar=1.0, in1=xg, op0=ALU.add,
                                         op1=ALU.mult).then_inc(sem("glu_step"), 1)
                dve.wait_ge(sem("glu_step"), i + 1)
                dve.wait_ge(sem("sigmoid"), i + 1)
                dve.tensor_tensor(act_rows, xl, sg, ALU.mult).then_inc(sem("act_ready"), 1)
                expert_column(nxt)
                add_rows(i)
            select_gates((n_items + (E - 1)) % E, n_items)
            add_rows(n_items)
            dve.wait_ge(sem("scat_added"), 8 * n_items + 9)
            scale_rows(("fin_norm",), hT, xT, "final", "h_fin", T)


_INS = ["x_prompt", "mem_prompt", "x_sample", "state_conformer_conv", "state_gdn_conv", "state_gdn", "cache_mem_k",
        "cache_mem_v", "w_in", "b_glu", "w_dw", "b_dw", "ln_g", "ln_b", "w_sc", "a_log", "dt_bias", "g_onorm",
        "w_out", "g_mix", "g_xattn", "g_mem", "w_xq", "w_mk", "w_mv", "w_xo", "g_moe", "w_router", "b_router",
        "w_gu", "b_gu", "w_dn", "b_dn", "g_final"]
_OUTS = [(1, 256, 1024), (8, 1, 1024), (1, 1, 30, 512), (1, 1, 3, 1536), (1, 1, 4, 128, 128), (1, 1, 256, 4, 256),
         (1, 1, 256, 4, 256), (1, 8, 30, 512), (1, 8, 3, 1536), (1, 8, 4, 128, 128)]


def kernel(**inputs):
    import numpy as _np
    import concourse.bacc as _bacc
    from concourse import mybir as _mybir
    from concourse.bass_utils import run_bass_kernel_spmd as _run

    nc = _bacc.Bacc("TRN2", target_bir_lowering=False, num_devices=1)
    arrays, args = {}, []
    for name in _INS:
        v = _np.ascontiguousarray(inputs[name])
        arrays[f"in_{name}"] = v
        args.append(nc.dram_tensor(f"in_{name}", v.shape, _mybir.dt.from_np(v.dtype), kind="ExternalInput").ap())
    outs = [nc.dram_tensor(f"out_{i}", s, _mybir.dt.float32, kind="ExternalOutput").ap()
            for i, s in enumerate(_OUTS)]
    bass_hymba_step(nc, args, outs)
    r = _run(nc, [arrays], core_ids=[0])
    return tuple(r.results[0][f"out_{i}"] for i in range(len(_OUTS)))
```
